# Optimizing a Trainium2 kernel written in Bass

```python
import math
import jax, jax.numpy as jnp
from jax import lax
import numpy as np

D_MODEL = 1024
BATCH = 1
SEQ = 256
DEPTH = 2

POOL_WINDOWS = (2, 4, 8, 16)
N_POOL_GROUPS = 4
POOL_GROUP_DIM = 64
POOL_WIDTH = N_POOL_GROUPS * POOL_GROUP_DIM
DIFF_HEADS = 6
DIFF_HEAD_DIM = 64
DIFF_V_DIM = 2 * DIFF_HEAD_DIM
DIFF_QK = 2 * DIFF_HEADS * DIFF_HEAD_DIM
DIFF_WIDTH = DIFF_HEADS * DIFF_V_DIM
DIFF_QBLOCK = 128
CONV_CH = 256
CONV_WIDTH = 31
MOBA_HEADS = 6
MOBA_HEAD_DIM = 128
MOBA_WIDTH = MOBA_HEADS * MOBA_HEAD_DIM
MOBA_BLOCK = 256
MOBA_TOPK = 3
MOBA_QCHUNK = 16
MIX_WIDTH = POOL_WIDTH + DIFF_WIDTH
AB_IN = POOL_WIDTH + 2 * DIFF_QK + DIFF_WIDTH
CD_IN = 2 * CONV_CH + 3 * MOBA_WIDTH
D_FF = -(-8 * D_MODEL // (3 * 256)) * 256
N_AB = (DEPTH + 1) // 2
N_CD = DEPTH // 2
EPS = 1e-6
NEG = -1e30

kernel_name = "hybrid_pool_diffattn_conformer_moba_trunk"

def rms_norm(x, g):
    x32 = x.astype(jnp.float32)
    y = x32 * lax.rsqrt(jnp.mean(jnp.square(x32), axis=-1, keepdims=True) + EPS)
    return (y * g).astype(x.dtype)

def layer_norm(x, g, b):
    x32 = x.astype(jnp.float32)
    mu = jnp.mean(x32, axis=-1, keepdims=True)
    var = jnp.mean(jnp.square(x32 - mu), axis=-1, keepdims=True)
    return ((x32 - mu) * lax.rsqrt(var + EPS) * g + b).astype(x.dtype)

def multiscale_pool(u, w_groups, scale):
    B_, S, _ = u.shape
    u32 = u.astype(jnp.float32)
    cs = jnp.cumsum(u32, axis=1)
    cs = jnp.concatenate([jnp.zeros_like(cs[:, :1]), cs], axis=1)
    pos = jnp.arange(S)
    outs = []
    for g, w in enumerate(POOL_WINDOWS):
        sl = slice(g * POOL_GROUP_DIM, (g + 1) * POOL_GROUP_DIM)
        c = cs[:, :, sl]
        upper = c[:, 1:]
        lower = jnp.pad(c, ((0, 0), (w - 1, 0), (0, 0)))[:, :S]
        cnt = jnp.minimum(pos + 1, w).astype(jnp.float32)[None, :, None]
        outs.append((upper - lower) / cnt - u32[:, :, sl])
    d = jnp.stack(outs, axis=2).astype(u.dtype)
    y = jnp.einsum('bsgc,gcd->bsgd', d, w_groups)
    return y.reshape(B_, S, POOL_WIDTH) * scale

def diff_attention(q, k, v, lam_params, subln_g, lam_init):
    B_, S = q.shape[:2]
    lp = lam_params.astype(jnp.float32)
    lam = jnp.exp(jnp.sum(lp[0] * lp[1])) - jnp.exp(jnp.sum(lp[2] * lp[3])) + lam_init
    kh = k.transpose(0, 2, 1, 3)
    vh = v.transpose(0, 2, 1, 3)
    nblk = S // DIFF_QBLOCK
    qb = q.reshape(B_, nblk, DIFF_QBLOCK, 2 * DIFF_HEADS, DIFF_HEAD_DIM).transpose(1, 0, 3, 2, 4)
    key_pos = jnp.arange(S)
    scale = DIFF_HEAD_DIM ** -0.5

    def block(args):
        q_blk, bi = args
        s = jnp.einsum('bhqd,bhkd->bhqk', q_blk, kh).astype(jnp.float32) * scale
        q_pos = bi * DIFF_QBLOCK + jnp.arange(DIFF_QBLOCK)
        s = jnp.where(key_pos[None, :] <= q_pos[:, None], s, NEG)
        p = jax.nn.softmax(s, axis=-1).reshape(B_, DIFF_HEADS, 2, DIFF_QBLOCK, S)
        a = p[:, :, 0] - lam * p[:, :, 1]
        return jnp.einsum('bhqk,bhkd->bhqd', a.astype(vh.dtype), vh)

    o = lax.map(block, (qb, jnp.arange(nblk)))
    o = rms_norm(o, subln_g) * (1.0 - lam_init)
    return o.transpose(1, 0, 3, 2, 4).reshape(B_, S, DIFF_WIDTH)

def conformer_conv(u, conv_w, conv_b, ln_g, ln_b):
    h = u[..., :CONV_CH] * jax.nn.sigmoid(u[..., CONV_CH:])
    h = lax.conv_general_dilated(
        h, conv_w[:, None, :], window_strides=(1,), padding=[(CONV_WIDTH - 1, 0)],
        dimension_numbers=('NWC', 'WIO', 'NWC'), feature_group_count=CONV_CH) + conv_b
    return jax.nn.silu(layer_norm(h, ln_g, ln_b))

def moba_attention(q, k, v):
    B_, S = q.shape[:2]
    Sp = -(-S // MOBA_BLOCK) * MOBA_BLOCK
    pad = ((0, 0), (0, Sp - S), (0, 0), (0, 0))
    q, k, v = [jnp.pad(t, pad).transpose(0, 2, 1, 3) for t in (q, k, v)]
    nb = Sp // MOBA_BLOCK
    topk = min(MOBA_TOPK, nb)
    k_blocks = k.reshape(B_, MOBA_HEADS, nb, MOBA_BLOCK, MOBA_HEAD_DIM)
    v_blocks = v.reshape(B_, MOBA_HEADS, nb, MOBA_BLOCK, MOBA_HEAD_DIM)
    k_mean = jnp.mean(k_blocks.astype(jnp.float32), axis=3).astype(k.dtype)
    nch = Sp // MOBA_QCHUNK
    qc = q.reshape(B_, MOBA_HEADS, nch, MOBA_QCHUNK, MOBA_HEAD_DIM).transpose(2, 0, 1, 3, 4)
    b_idx = jnp.arange(B_)[:, None, None, None]
    h_idx = jnp.arange(MOBA_HEADS)[None, :, None, None]
    blk_ids = jnp.arange(nb)
    own_off = jnp.arange(MOBA_BLOCK)
    scale = MOBA_HEAD_DIM ** -0.5

    def chunk(args):
        q_c, ci = args
        start = ci * MOBA_QCHUNK
        i = start // MOBA_BLOCK
        q_pos = start + jnp.arange(MOBA_QCHUNK)
        gate = jnp.einsum('bhqd,bhnd->bhqn', q_c, k_mean).astype(jnp.float32)
        gate = jnp.where(blk_ids < i, gate, NEG)
        _, idx = lax.top_k(gate, topk)
        valid = idx < i
        k_sel = k_blocks[b_idx, h_idx, idx]
        v_sel = v_blocks[b_idx, h_idx, idx]
        s_sel = jnp.einsum('bhqd,bhqjkd->bhqjk', q_c, k_sel).astype(jnp.float32) * scale
        s_sel = jnp.where(valid[..., None], s_sel, NEG).reshape(B_, MOBA_HEADS, MOBA_QCHUNK, topk * MOBA_BLOCK)
        k_own = lax.dynamic_slice_in_dim(k, i * MOBA_BLOCK, MOBA_BLOCK, axis=2)
        v_own = lax.dynamic_slice_in_dim(v, i * MOBA_BLOCK, MOBA_BLOCK, axis=2)
        s_own = jnp.einsum('bhqd,bhkd->bhqk', q_c, k_own).astype(jnp.float32) * scale
        s_own = jnp.where(i * MOBA_BLOCK + own_off[None, :] <= q_pos[:, None], s_own, NEG)
        p = jax.nn.softmax(jnp.concatenate([s_sel, s_own], axis=-1), axis=-1)
        p_sel = p[..., :topk * MOBA_BLOCK].reshape(B_, MOBA_HEADS, MOBA_QCHUNK, topk, MOBA_BLOCK).astype(v.dtype)
        p_own = p[..., topk * MOBA_BLOCK:].astype(v.dtype)
        return (jnp.einsum('bhqjk,bhqjkd->bhqd', p_sel, v_sel)
                + jnp.einsum('bhqk,bhkd->bhqd', p_own, v_own))

    o = lax.map(chunk, (qc, jnp.arange(nch)))
    return o.transpose(1, 0, 3, 2, 4).reshape(B_, Sp, MOBA_WIDTH)[:, :S]

def setup_inputs(seed: int = 0) -> dict:
    key = jax.random.key(seed)
    ks = jax.random.split(key, 20)
    f32 = jnp.float32

    def nrm(k, shape, s):
        return jax.random.normal(k, shape, f32) * s

    return {
        "x": nrm(ks[0], (BATCH, SEQ, D_MODEL), 1.0),
        "norm_mix_g": 1.0 + nrm(ks[1], (DEPTH, D_MODEL), 0.02),
        "norm_ffn_g": 1.0 + nrm(ks[2], (DEPTH, D_MODEL), 0.02),
        "norm_final_g": 1.0 + nrm(ks[3], (D_MODEL,), 0.02),
        "ab_w_in": nrm(ks[4], (N_AB, D_MODEL, AB_IN), D_MODEL ** -0.5),
        "ab_w_out": nrm(ks[5], (N_AB, MIX_WIDTH, D_MODEL), MIX_WIDTH ** -0.5),
        "pool_w": nrm(ks[6], (N_AB, N_POOL_GROUPS, POOL_GROUP_DIM, POOL_GROUP_DIM), POOL_GROUP_DIM ** -0.5),
        "pool_scale": 1.0 + nrm(ks[7], (N_AB, POOL_WIDTH), 0.02),
        "diff_lambda": nrm(ks[8], (N_AB, 4, DIFF_HEAD_DIM), 0.1),
        "diff_subln_g": 1.0 + nrm(ks[9], (N_AB, DIFF_V_DIM), 0.02),
        "cd_w_in": nrm(ks[10], (N_CD, D_MODEL, CD_IN), D_MODEL ** -0.5),
        "cd_w_out": nrm(ks[11], (N_CD, MIX_WIDTH, D_MODEL), MIX_WIDTH ** -0.5),
        "conv_w": nrm(ks[12], (N_CD, CONV_WIDTH, CONV_CH), CONV_WIDTH ** -0.5),
        "conv_b": nrm(ks[13], (N_CD, CONV_CH), 0.02),
        "conv_ln_g": 1.0 + nrm(ks[14], (N_CD, CONV_CH), 0.02),
        "conv_ln_b": nrm(ks[15], (N_CD, CONV_CH), 0.02),
        "ffn_w_gate": nrm(ks[16], (DEPTH, D_MODEL, D_FF), D_MODEL ** -0.5),
        "ffn_w_up": nrm(ks[17], (DEPTH, D_MODEL, D_FF), D_MODEL ** -0.5),
        "ffn_w_down": nrm(ks[18], (DEPTH, D_FF, D_MODEL), D_FF ** -0.5),
    }

def reference(x, norm_mix_g, norm_ffn_g, norm_final_g, ab_w_in, ab_w_out, pool_w, pool_scale,
              diff_lambda, diff_subln_g, cd_w_in, cd_w_out, conv_w, conv_b, conv_ln_g, conv_ln_b,
              ffn_w_gate, ffn_w_up, ffn_w_down):
    B_, S, _ = x.shape
    h = x
    for layer in range(DEPTH):
        xn = rms_norm(h, norm_mix_g[layer])
        j = layer // 2
        if layer % 2 == 0:
            proj = xn @ ab_w_in[j]
            o = POOL_WIDTH
            u_pool = proj[..., :o]
            q = proj[..., o:o + DIFF_QK].reshape(B_, S, 2 * DIFF_HEADS, DIFF_HEAD_DIM)
            k = proj[..., o + DIFF_QK:o + 2 * DIFF_QK].reshape(B_, S, 2 * DIFF_HEADS, DIFF_HEAD_DIM)
            v = proj[..., o + 2 * DIFF_QK:].reshape(B_, S, DIFF_HEADS, DIFF_V_DIM)
            lam_init = 0.8 - 0.6 * math.exp(-0.3 * layer)
            y_a = multiscale_pool(u_pool, pool_w[j], pool_scale[j])
            y_b = diff_attention(q, k, v, diff_lambda[j], diff_subln_g[j], lam_init)
            mix = jnp.concatenate([y_a, y_b], axis=-1) @ ab_w_out[j]
        else:
            proj = xn @ cd_w_in[j]
            o = 2 * CONV_CH
            u_conv = proj[..., :o]
            q = proj[..., o:o + MOBA_WIDTH].reshape(B_, S, MOBA_HEADS, MOBA_HEAD_DIM)
            k = proj[..., o + MOBA_WIDTH:o + 2 * MOBA_WIDTH].reshape(B_, S, MOBA_HEADS, MOBA_HEAD_DIM)
            v = proj[..., o + 2 * MOBA_WIDTH:].reshape(B_, S, MOBA_HEADS, MOBA_HEAD_DIM)
            y_c = conformer_conv(u_conv, conv_w[j], conv_b[j], conv_ln_g[j], conv_ln_b[j])
            y_d = moba_attention(q, k, v)
            mix = jnp.concatenate([y_c, y_d], axis=-1) @ cd_w_out[j]
        h = h + mix
        hn = rms_norm(h, norm_ffn_g[layer])
        h = h + (jax.nn.silu(hn @ ffn_w_gate[layer]) * (hn @ ffn_w_up[layer])) @ ffn_w_down[layer]
    return rms_norm(h, norm_final_g)


_drawn_inputs = setup_inputs


def setup_inputs(seed=0):
    import zlib

    import numpy as np

    out = dict(_drawn_inputs(seed))
    spreads = {}
    factors = {'norm_ffn_g': 3.253,
     'norm_final_g': 3.013,
     'pool_scale': 7.182,
     'diff_subln_g': 3.933,
     'conv_b': 5.781,
     'conv_ln_g': 8.0,
     'conv_ln_b': 8.0}
    for name, (base, spread) in spreads.items():
        noise = np.random.default_rng([zlib.crc32(name.encode()), seed]).standard_normal(out[name].shape)
        drawn = base * np.exp(spread * noise) if base else spread * noise
        out[name] = __import__('jax').numpy.asarray(drawn.astype(out[name].dtype))
    for name, factor in factors.items():
        out[name] = (out[name] * factor).astype(out[name].dtype)
    return out
```

```python
import math
from contextlib import ExitStack

import concourse.bass as bass
from concourse import mybir

F32 = mybir.dt.float32
F32R = mybir.dt.float32r
BF16 = mybir.dt.bfloat16
ALU = mybir.AluOpType
ACT = mybir.ActivationFunctionType
AX_X = mybir.AxisListType.X

P = 128
HALVES = 2
EPS = 1e-6
NEG = -1e30
POOL_WINDOWS = (2, 4, 8, 16)
LAM_INIT = 0.8 - 0.6 * math.exp(-0.3 * 0)

SLAB = 2048
RAW_SLOTS = 3
SLOTS = 6
LOADS = 2

SCORE_BANKS = ((0, 1, 2), (0, 1, 2), (6, 4, 5))
PROB_T_BANKS = ((6, 7), (6, 3), (7, 4))
OUT_BANK = (3, 7, 5)
Y_BANK = (3, 7, 6)


def trunk(nc, x, norm_mix_g, norm_ffn_g, norm_final_g, ab_w_in, ab_w_out, pool_w, diff_lambda,
          diff_subln_g, cd_w_in, cd_w_out, channel_params, ffn_w_gate, ffn_w_up, ffn_w_down, out):
    SEQ, D = x.shape
    KC = D // P
    POOL = pool_w.shape[1] * pool_w.shape[0]
    DFF = ffn_w_gate.shape[2]
    TAPS = channel_params.shape[1] - 4
    CONV = channel_params.shape[0]
    HEADS = 6
    HD = 128
    WIDTH = HEADS * HD
    NCH = DFF // 256
    HALFD = D // 2
    assert SEQ == 2 * P and D == 1024 and DFF % 256 == 0 and POOL == 256 and CONV == 256

    NAT = (4, 5)
    mix0 = [0, NAT[0] + 6 + 4 + 3 * NCH]
    out0 = [mix0[l] + NAT[l] + 6 for l in range(2)]
    ffn0 = [out0[l] + 4 for l in range(2)]
    SLABS = ffn0[1] + 3 * NCH

    OUT_ROWS = ((0, 2, 4, 6), (2, 4, 6, 0))

    def unit_no(i, half):
        return 2 * half + i if i < 2 else 2 * i + half

    def up_slab(l, i):
        return ffn0[l] + 2 * i if not in_register(i) and i < 2 else ffn0[l] + 3 * i - 1

    def down_slab(l, i):
        return ffn0[l] + 3 * i + (4 if in_register(i) or i < NCH - 1 else 2)

    def in_register(i):
        return not isinstance(i, int)

    ctx = ExitStack()
    with ctx:
        def sb(name, shape, dt=F32):
            return ctx.enter_context(nc.sbuf_tensor(name, shape, dt))

        def sem(name):
            return ctx.enter_context(nc.semaphore(name))

        raw = sb("raw", [P, RAW_SLOTS, SLAB])
        w_hi = sb("w_hi", [P, SLOTS, SLAB], F32R)
        w_lo = sb("w_lo", [P, SLOTS, SLAB], F32R)
        xT_hi = sb("xT_hi", [P, HALVES, KC, P], F32R)
        xT_lo = sb("xT_lo", [P, HALVES, KC, P], F32R)
        yT_hi = sb("yT_hi", [P, HALVES, KC, P], F32R)
        yT_lo = sb("yT_lo", [P, HALVES, KC, P], F32R)
        h = sb("h", [P, HALVES, D])
        xn = sb("xn", [P, D])
        gain = sb("gain", [P, D])
        v = sb("v", [P, HALVES, WIDTH])
        qT = sb("qT", [P, 2, SEQ])
        kT = sb("kT", [P, 2, 2, SEQ])
        work = sb("work", [P, 12, P])
        probT = sb("probT", [P, 2, 3, P])
        o_sb = sb("o_sb", [P, HALVES, 2, P])
        branch = sb("branch", [P, 4, 3 * P])
        u_sb = sb("u_sb", [P, HALVES, POOL])
        pw_sb = sb("pw_sb", [64, 4, 64])
        chan = sb("chan", [P, 2, TAPS + 4])
        chan_half = sb("chan_half", [P, 2, 2])
        subg = sb("subg", [P, HD])
        lam_in = sb("lam_in", [P, 4, 64])
        ident = sb("ident", [P, P])
        ident_b = sb("ident_b", [P, P], BF16)
        mask_b = sb("mask_b", [P, P], BF16)
        sumsq = sb("sumsq", [P, 4])
        power = sb("power", [P, 4])
        meansq = sb("meansq", [P, 4])
        rstd = sb("rstd", [P, 4])
        rmax = sb("rmax", [P, 8])
        nmax = sb("nmax", [P, 8])
        sums = sb("sums", [P, 8])
        coef = sb("coef", [P, 8])
        rsum = sb("rsum", [P, 8])
        osq = sb("osq", [P, 4])
        lam_t = sb("lam_t", [P, 4])
        stats = sb("stats", [P, HALVES, 6])
        mv = sb("mv", [P, HALVES, 2])
        bank = ctx.enter_context(nc.psum_tensor("bank", [P, 8, 512], F32))

        p0 = work[:, 0:4, :]
        p1 = work[:, 4:12, :].rearrange("p (m b) k -> p m (b k)", b=2)
        tmp_t = work[:, 0:4, :].rearrange("p (n b) k -> p n (b k)", b=2)
        tmp_a = work[:, 4:8, :].rearrange("p (n b) k -> p n (b k)", b=2)
        actT_hi = yT_hi[:, :, 0:4, :]
        actT_lo = yT_lo[:, :, 0:4, :]
        dT = xn[0:64, :].rearrange("p (g t) -> p g t", g=4)
        PAD = TAPS - 1
        conv_in = branch[:, 0:2, 0:PAD + SEQ]
        conv_acc = branch[:, 2:4, 0:SEQ]

        x_loaded = [sem(f"x_loaded{i}") for i in range(HALVES)]
        gain_loaded = sem("gain_loaded")
        params_loaded = sem("params_loaded")
        out_stored = sem("out_stored")
        raw_loaded = [sem(f"raw_loaded{i}") for i in range(RAW_SLOTS)]
        hi_ready = sem("hi_ready")
        lo_ready = sem("lo_ready")
        slab_used = sem("slab_used")
        consts = sem("consts")
        h_added = sem("h_added")
        squared = sem("squared")
        eps_added = sem("eps_added")
        pow_asked = sem("pow_asked")
        pow_done = sem("pow_done")
        normed = sem("normed")
        normed_t = sem("normed_t")
        xt_hi = sem("xt_hi")
        xt_lo = sem("xt_lo")
        nat_done = sem("nat_done")
        nat_copied = sem("nat_copied")
        q_done = sem("q_done")
        q_copied = sem("q_copied")
        k_copied = sem("k_copied")
        scored = sem("scored")
        nmax_ready = sem("nmax_ready")
        exp_done = sem("exp_done")
        probs_ready = sem("probs_ready")
        prob_t = sem("prob_t")
        probT_a = sem("probT_a")
        probT_b = sem("probT_b")
        o_done = sem("o_done")
        o_squared = sem("o_squared")
        o_ready = sem("o_ready")
        o_scaled = sem("o_scaled")
        recip_ready = sem("recip_ready")
        y_t = sem("y_t")
        y_hi = sem("y_hi")
        y_lo = sem("y_lo")
        branch_t = sem("branch_t")
        branch_act = sem("branch_act")
        branch_dve = sem("branch_dve")
        branch_lo = sem("branch_lo")
        conv_step = sem("conv_step")
        lam_exp = sem("lam_exp")
        up_done = sem("up_done")
        tanh_done = sem("tanh_done")
        gated = sem("gated")
        act_ready = sem("act_ready")
        act_t = sem("act_t")
        at_hi = sem("at_hi")
        at_lo = sem("at_lo")
        acc_done = sem("acc_done")
        dve_chain = sem("dve_chain")

        POWS = ([("norm", 0, 0), ("norm", 0, 1)] + [("head", j, 0) for j in range(3)]
                + [("norm", st, hf) for st in (1, 2) for hf in range(2)]
                + [("ln", 0, 0)] + [("norm", st, hf) for st in (3, 4) for hf in range(2)])

        def pow_no(kind, a, b=0):
            return POWS.index((kind, a, b)) + 1

        def slot(s):
            return s % SLOTS

        block = ctx.enter_context(nc.Block())

        @block.sync
        def _(sp):
            def into_slot(s):
                if in_register(s) or s >= RAW_SLOTS:
                    sp.wait_ge(lo_ready, s - RAW_SLOTS + 1)

            def load_columns(s, parts, k0, nk, static_slot):
                into_slot(s)
                width = sum(w for _, _, w in parts)
                dst = raw[:, static_slot % RAW_SLOTS, 0:nk * width].rearrange("p (k n) -> p k n", k=nk)
                at = 0
                for m, c0, w in parts:
                    src = m[k0 * P:(k0 + nk) * P, bass.ds(c0, w)].rearrange("(k p) n -> p k n", p=P)
                    sp.dma_start(dst[:, :, at:at + w], src).then_inc(raw_loaded[static_slot % RAW_SLOTS], 16)
                    at += w

            def load_rows(s, m, row0, static_slot):
                into_slot(s)
                for k in range(2):
                    sp.dma_start(raw[:, static_slot % RAW_SLOTS, k * D:(k + 1) * D],
                                 m[bass.ds(row0 + k * P, P), :]).then_inc(raw_loaded[static_slot % RAW_SLOTS], 16)

            def two(m, c0, w):
                return [(m, c0, w // 2), (m, c0 + w // 2, w // 2)]

            def load_gain(st):
                g = [norm_mix_g[0:1, :], norm_ffn_g[0:1, :], norm_mix_g[1:2, :], norm_ffn_g[1:2, :],
                     norm_final_g][st]
                if st:
                    sp.wait_ge(normed, 4 * st)
                sp.dma_start(gain[:, :], g.broadcast_to([P, D]))\
                  .then_inc(gain_loaded, 16)

            def load_mix_in(l):
                w = (ab_w_in, cd_w_in)[l]
                s = mix0[l]
                c_v = POOL + 2 * WIDTH if l == 0 else 2 * CONV + 2 * WIDTH
                c_q = POOL if l == 0 else 2 * CONV
                c_k = c_q + WIDTH
                if l == 0:
                    units = [[(w, 0, POOL), (w, c_v, 256)], two(w, c_v + 256, 512)]
                else:
                    units = [[(w, 0, CONV), (w, CONV, CONV)], two(w, c_v, 512)]
                for u in units:
                    if s == 2:
                        load_x(1)
                        load_params()
                    for k0 in (0, 4):
                        load_columns(s, u, k0, 4, s)
                        s += 1
                if l == 1:
                    load_columns(s, two(w, c_v + 512, 256), 0, 8, s)
                    s += 1
                for j in range(3):
                    for k0 in (0, 4):
                        load_columns(s, [(w, c_q + 256 * j, 256), (w, c_k + 256 * j, 256)], k0, 4, s)
                        s += 1

            def load_params():
                for dst, src in ((pw_sb[:, :, :], pool_w.rearrange("g c d -> c g d")),
                                 (chan[:, :, :], channel_params.rearrange("(c p) n -> p c n", p=P)),
                                 (subg[:, :], diff_subln_g.broadcast_to([P, HD])),
                                 (lam_in[:, :, :].rearrange("p a b -> p (a b)"),
                                  diff_lambda.rearrange("a b -> (a b)").rearrange("(o n) -> o n", o=1)
                                  .broadcast_to([P, 256]))):
                    sp.dma_start(dst, src).then_inc(params_loaded, 16)

            def load_ffn(l):
                def up(i, par):
                    s = up_slab(l, i)
                    for a in range(2):
                        load_columns(s + a, [(ffn_w_gate[l], i * 256, 256), (ffn_w_up[l], i * 256, 256)],
                                     4 * a, 4, par + a)

                def down(i, par):
                    load_rows(down_slab(l, i), ffn_w_down[l], i * 256, par)

                for i in range(2):
                    up(i, up_slab(l, i))
                down(0, down_slab(l, 0))
                with sp.Fori(2, NCH) as i:
                    up(i, up_slab(l, 2))
                    down(i - 1, down_slab(l, 1))
                down(NCH - 1, down_slab(l, NCH - 1))

            def load_x(half):
                sp.dma_start(h[:, half, :], x[half * P:(half + 1) * P, :]).then_inc(x_loaded[half], 16)

            load_x(0)
            load_gain(0)
            for l in range(2):
                load_mix_in(l)
                load_gain(2 * l + 1)
                for o in range(4):
                    load_rows(out0[l] + o, (ab_w_out, cd_w_out)[l], OUT_ROWS[l][o] * P, out0[l] + o)
                load_ffn(l)
                load_gain(2 * l + 2)
            for half in range(HALVES):
                sp.wait_ge(normed, 16 + 2 * half + 2)
                sp.dma_start(out[half * P:(half + 1) * P, :], h[:, half, :]).then_inc(out_stored, 16)
            sp.wait_ge(out_stored, 16 * HALVES)

        @block.gpsimd
        def _(pool):
            made = [0]

            def step(ins):
                made[0] += 1
                ins.then_inc(consts, 1)
                pool.wait_ge(consts, made[0])

            step(nc.gpsimd.memset(power[:, :], -0.5))
            step(nc.gpsimd.memset(ident[:, :], 0.0))
            step(nc.gpsimd.affine_select(out=ident[:, :], in_=ident[:, :], compare_op=ALU.not_equal, fill=1.0,
                                         base=0, pattern=[[-1, P]], channel_multiplier=1))
            IDENT_MADE = made[0]
            assert IDENT_MADE == 3
            for half in range(HALVES):
                pool.wait_ge(pow_asked, half + 1)
                nc.gpsimd.tensor_tensor(rstd[:, half:half + 1], meansq[:, half:half + 1],
                                        power[:, 0:1], ALU.pow).then_inc(pow_done, 1)
            step(nc.gpsimd.tensor_copy(ident_b[:, :], ident[:, :]))
            step(nc.gpsimd.memset(mask_b[:, :], 0.0))
            step(nc.gpsimd.affine_select(out=mask_b[:, :], in_=mask_b[:, :], compare_op=ALU.is_ge, fill=NEG,
                                         base=0, pattern=[[-1, P]], channel_multiplier=1))
            for g, w in enumerate(POOL_WINDOWS):
                step(nc.gpsimd.memset(branch[:, g, :], 1.0 / w))
                for t in range(w - 1):
                    step(nc.gpsimd.memset(branch[:, g, t:t + 1], 1.0 / (t + 1)))
                for c0, n in ((0, 2 * P), (2 * P, P)):
                    b = branch[:, g, c0:c0 + n]
                    step(nc.gpsimd.affine_select(out=b, in_=b, compare_op=ALU.is_ge, fill=0.0, base=0,
                                                 pattern=[[1, n]], channel_multiplier=-1))
                    step(nc.gpsimd.affine_select(out=b, in_=b, compare_op=ALU.is_ge, fill=0.0, base=w - 1,
                                                 pattern=[[-1, n]], channel_multiplier=1))
                    d = branch[:, g, c0:c0 + P]
                    step(nc.gpsimd.tensor_tensor(d, d, ident[:, :], ALU.subtract))
            assert made[0] == CONSTS_MADE
            for n, (kind, a, b) in enumerate(POWS):
                if n < 2:
                    continue
                pool.wait_ge(pow_asked, n + 1)
                if kind == "norm":
                    o, i, e = rstd[:, b:b + 1], meansq[:, b:b + 1], power[:, 0:1]
                elif kind == "head":
                    o, i, e = osq[:, :], osq[:, :], power[:, :]
                else:
                    o, i, e = rstd[:, 2:4], meansq[:, 2:4], power[:, 0:2]
                nc.gpsimd.tensor_tensor(o, i, e, ALU.pow).then_inc(pow_done, 1)

        @block.scalar
        def _(act):
            A = nc.scalar.activation

            def split_hi(s, static_slot=None, turn=None):
                t = s if static_slot is None else static_slot
                act.wait_ge(raw_loaded[t % RAW_SLOTS],
                            16 * LOADS * (s // RAW_SLOTS + 1) if turn is None else turn)
                if static_slot is not None or s >= SLOTS:
                    act.wait_ge(slab_used, s - SLOTS + 1)
                A(w_hi[:, t % SLOTS, :], raw[:, t % RAW_SLOTS, :], ACT.Copy).then_inc(hi_ready, 1)

            def split_his(*slabs):
                for s in slabs:
                    if s < SLABS:
                        split_hi(s)

            def norm_squares(st, half):
                for b in range(2):
                    if st == 0:
                        if b == 0:
                            act.wait_ge(x_loaded[half], 16)
                    else:
                        act.wait_ge(h_added, 4 * (st - 1) + 2 * half + b + 1)
                    if b == 1 or half == 1 or st > 0:
                        act.wait_ge(squared, 4 * st + 2 * half + b)
                    A(xn[:, b * HALFD:(b + 1) * HALFD], h[:, half, b * HALFD:(b + 1) * HALFD], ACT.Square,
                      accum_out=sumsq[:, 2 * half + b:2 * half + b + 1]).then_inc(squared, 1)

            def norm_hi(st, half):
                for b in range(2):
                    act.wait_ge(normed_t, 4 * st + 2 * half + b + 1)
                    A(xT_hi[:, half, 4 * b:4 * b + 4, :].rearrange("p k t -> p (k t)"), bank[:, 6 + b, :],
                      ACT.Copy).then_inc(xt_hi, 1)

            def q_evac(g):
                l, j = divmod(g, 3)
                act.wait_ge(q_done, g + 1)
                last = A(qT[:, :, :].rearrange("p s t -> p (s t)"), bank[:, 4, :], ACT.Copy)
                if l == 1:
                    act.wait_ge(slab_used, mix0[l] + NAT[l] + 2 * j + 2)
                    last = A(kT[:, 0, :, :].rearrange("p s t -> p (s t)"), bank[:, 5, :], ACT.Copy)
                last.then_inc(q_copied, 1)

            def exps(l, j):
                g, maps = 3 * l + j, 4 if l == 0 else 2
                scale = float(64 if l == 0 else 128) ** -0.5
                b0, *b1 = SCORE_BANKS[j]
                act.wait_ge(nmax_ready, g + 1)
                for m in range(maps):
                    A(p0[:, m, :], bank[:, b0, m * P:(m + 1) * P], ACT.Exp, bias=nmax[:, m:m + 1],
                      scale=scale, accum_out=sums[:, m:m + 1])
                for m in range(maps):
                    c = (m % 2) * 256
                    last = A(p1[:, m, :], bank[:, b1[m // 2], c:c + 256], ACT.Exp,
                             bias=nmax[:, 4 + m:5 + m], scale=scale, accum_out=sums[:, 4 + m:5 + m])
                last.then_inc(exp_done, 1)

            def probT_evac(l, j):
                g = 3 * l + j
                for hd in range(1 + l):
                    act.wait_ge(prob_t, 2 * g + hd + 1)
                    A(probT[:, hd, :, :].rearrange("p b q -> p (b q)"), bank[:, PROB_T_BANKS[j][hd], 0:3 * P],
                      ACT.Copy).then_inc(probT_a, 1)

            def o_scale(j):
                act.wait_ge(o_done, 3 + j + 1)
                act.wait_ge(recip_ready, j + 1)
                for i in range(4):
                    c = 4 * (i // 2) + i % 2
                    last = A(o_sb[:, i // 2, i % 2, :], bank[:, OUT_BANK[j], i * P:(i + 1) * P], ACT.Copy,
                             scale=rsum[:, c:c + 1])
                last.then_inc(o_scaled, 1)

            def o_squares(j):
                act.wait_ge(o_done, j + 1)
                for i in range(4):
                    last = A(o_sb[:, i // 2, i % 2, :], bank[:, OUT_BANK[j], i * P:(i + 1) * P], ACT.Square,
                             accum_out=osq[:, i:i + 1])
                last.then_inc(o_squared, 1)

            def y_hi_evac(l, j):
                act.wait_ge(y_t, 3 * l + j + 1)
                A(yT_hi[:, :, 2 + 2 * j:4 + 2 * j, :],
                  bank[:, Y_BANK[j], :].rearrange("p (h k t) -> p h k t", h=2, k=2), ACT.Copy).then_inc(y_hi, 1)

            def mix0_act():
                for half in range(HALVES):
                    act.wait_ge(*((nat_done, 1) if half == 0 else (slab_used, 2)))
                    A(u_sb[:, half, :], bank[:, 4, 0:POOL], ACT.Copy)
                    A(v[:, half, 0:256], bank[:, 4, 256:512], ACT.Copy).then_inc(nat_copied, 1)
                    act.wait_ge(*((nat_done, 2) if half == 0 else (slab_used, 4)))
                    A(v[:, half, 256:768], bank[:, 5, :], ACT.Copy).then_inc(nat_copied, 1)
                    if half == 0:
                        split_his(4, 5)
                act.wait_ge(lam_exp, 1)
                A(lam_t[:, 2:4], lam_t[:, 0:2], ACT.Exp).then_inc(lam_exp, 1)
                split_his(6, 7)
                q_evac(0)
                for i in range(2):
                    act.wait_ge(branch_t, i + 1)
                    A(dT[:, 2 * i:2 * i + 2, :].rearrange("p g t -> p (g t)"), bank[0:64, 6 + i, :], ACT.Copy)\
                        .then_inc(branch_act, 1)
                split_his(8, 9)
                exps(0, 0)
                act.wait_ge(branch_t, 3)
                for c in range(2):
                    A(yT_hi[:, :, c, :], bank[:, 3, c * 256:(c + 1) * 256].rearrange("p (h t) -> p h t", h=2),
                      ACT.Copy, scale=chan[:, c, TAPS + 3:TAPS + 4]).then_inc(branch_act, 1)
                split_his(10, 11)
                q_evac(1)
                probT_evac(0, 0)
                o_squares(0)
                split_his(12)
                exps(0, 1)
                split_his(13)
                q_evac(2)
                y_hi_evac(0, 0)
                probT_evac(0, 1)
                o_squares(1)
                split_his(14)
                exps(0, 2)
                split_his(15)
                y_hi_evac(0, 1)
                split_his(16)
                probT_evac(0, 2)
                o_squares(2)
                y_hi_evac(0, 2)
                split_his(17)

            def mix1_act():
                m = mix0[1]
                o = out0[1]
                for half in range(HALVES):
                    act.wait_ge(*((nat_done, 3) if half == 0 else (slab_used, m + 2)))
                    A(tmp_t[:, half, :], bank[:, 4, 256:512], ACT.Tanh, scale=0.5).then_inc(branch_act, 1)
                    act.wait_ge(*((nat_done, 4) if half == 0 else (slab_used, m + 4)))
                    A(v[:, half, 0:512], bank[:, 5, :], ACT.Copy).then_inc(nat_copied, 1)
                act.wait_ge(branch_t, 4)
                A(conv_in[:, :, PAD:PAD + SEQ], bank[:, 6, :].rearrange("p (c t) -> p c t", c=2), ACT.Copy,
                  scale=0.5).then_inc(branch_act, 1)
                split_his(m + 6)
                for half in range(HALVES):
                    act.wait_ge(*((nat_done, 5) if half == 0 else (slab_used, m + 5)))
                    A(v[:, half, 512:768], bank[:, 4 + half, 0:256], ACT.Copy).then_inc(nat_copied, 1)
                split_his(m + 7, m + 8)
                q_evac(3)
                split_his(m + 9)
                exps(1, 0)
                split_his(m + 10)
                q_evac(4)
                probT_evac(1, 0)
                o_scale(0)
                split_his(o)
                exps(1, 1)
                split_his(o + 1)
                q_evac(5)
                y_hi_evac(1, 0)
                probT_evac(1, 1)
                o_scale(1)
                split_his(o + 2)
                exps(1, 2)
                split_his(o + 3, ffn0[1])
                y_hi_evac(1, 1)
                split_his(ffn0[1] + 1)
                probT_evac(1, 2)
                o_scale(2)
                y_hi_evac(1, 2)
                split_his(ffn0[1] + 2)
                act.wait_ge(branch_t, 6)
                for c in range(2):
                    A(conv_in[:, c, 0:SEQ], bank[:, 4, c * 256:(c + 1) * 256], ACT.Tanh,
                      bias=chan_half[:, c, 1:2], scale=chan_half[:, c, 0:1]).then_inc(branch_act, 1)
                act.wait_ge(branch_dve, BR_CONV_W)
                A(yT_hi[:, :, 0:2, :].rearrange("p h c t -> p c h t"),
                  conv_acc.rearrange("p c (h t) -> p c h t", h=2), ACT.Copy, scale=0.5).then_inc(branch_act, 1)
                split_his(ffn0[1] + 3)

            def ffn_act(l):
                U = 22 * l

                def tanh(i, half, p):
                    if half == 0:
                        act.wait_ge(up_done, NCH * l + i + 1)
                    else:
                        act.wait_ge(slab_used, up_slab(l, i) + 2)
                    A(tmp_t[:, p, :], bank[:, 4 + p, 0:256], ACT.Tanh, scale=0.5).then_inc(tanh_done, 1)

                def at_hi_evac(n, p, ip, half):
                    act.wait_ge(act_t, U + n + 1)
                    A(actT_hi[:, half, 2 * ip:2 * ip + 2, :].rearrange("p k t -> p (k t)"),
                      bank[:, 6 + p, 0:256], ACT.Copy).then_inc(at_hi, 1)

                f = ffn0[l]
                norm_squares(2 * l + 1, 0)
                norm_hi(2 * l + 1, 0)
                split_his(f + 4)
                norm_squares(2 * l + 1, 1)
                tanh(0, 0, 0)
                norm_hi(2 * l + 1, 1)
                split_his(f + 5)
                tanh(1, 0, 1)
                at_hi_evac(0, 0, 0, 0)
                tanh(0, 1, 0)
                split_his(f + 6, f + 7)
                at_hi_evac(1, 1, 1, 0)
                tanh(1, 1, 1)
                at_hi_evac(2, 0, 0, 1)

                def chunk(i, p):
                    s, static = up_slab(l, i) + 3, up_slab(l, 2 + p) + 3

                    def split(a):
                        first = (static + a) // RAW_SLOTS + 1
                        split_hi(s + a, static + a, 16 * LOADS * (i + (first - 2 - p)))

                    split(0)
                    tanh(i, 0, 0)
                    at_hi_evac(2 * i - 1, 1, 1 - p, 1)
                    split(1)
                    tanh(i, 1, 1)
                    at_hi_evac(2 * i, 0, p, 0)
                    split(2)

                with act.Fori(2, NCH - 1, 2) as i:
                    chunk(i, 0)
                    chunk(i + 1, 1)
                last = NCH - 1
                nxt = f + 3 * NCH
                split_his(nxt - 1)
                tanh(last, 0, 0)
                at_hi_evac(2 * last - 1, 1, 1 - last % 2, 1)
                split_his(nxt)
                tanh(last, 1, 1)
                at_hi_evac(2 * last, 0, last % 2, 0)
                split_his(nxt + 1)
                at_hi_evac(2 * last + 1, 1, last % 2, 1)
                split_his(nxt + 2, nxt + 3)

            norm_squares(0, 0)
            split_his(0)
            norm_hi(0, 0)
            norm_squares(0, 1)
            split_his(1, 2, 3)
            norm_hi(0, 1)
            mix0_act()
            ffn_act(0)
            norm_squares(2, 0)
            norm_hi(2, 0)
            split_his(mix0[1] + 4)
            norm_squares(2, 1)
            norm_hi(2, 1)
            split_his(mix0[1] + 5)
            mix1_act()
            ffn_act(1)
            norm_squares(4, 0)
            norm_squares(4, 1)

        @block.vector
        def _(dve):
            V = nc.vector
            chain = [0]

            def link(ins):
                chain[0] += 1
                ins.then_inc(dve_chain, 1)
                dve.wait_ge(dve_chain, chain[0])

            def split_lo(s, static=None):
                t = s if static is None else static
                dve.wait_ge(hi_ready, s + 1)
                V.tensor_tensor(w_lo[:, t % SLOTS, :], raw[:, t % RAW_SLOTS, :],
                                w_hi[:, t % SLOTS, :].bitcast(F32), ALU.subtract).then_inc(lo_ready, 1)

            def split_los(*slabs):
                for s in slabs:
                    if s < SLABS:
                        split_lo(s)

            def norm_add(st, half):
                for b in range(2):
                    if half and b:
                        dve.wait_ge(slab_used, (ffn0[0], mix0[1], ffn0[1], SLABS)[st - 1])
                    else:
                        dve.wait_ge(acc_done, 3 * (st - 1) + 2 * half + b + 1)
                    hp = h[:, half, b * HALFD:(b + 1) * HALFD]
                    V.tensor_tensor(hp, bank[:, 2 * half + b, :], hp, ALU.add).then_inc(h_added, 1)

            def norm_scale(st, half):
                n = 4 * st + 2 * half
                dve.wait_ge(squared, n + 1)
                link(V.tensor_scalar(meansq[:, half:half + 1], sumsq[:, 2 * half:2 * half + 1],
                                     D * EPS, None, ALU.add))
                dve.wait_ge(squared, n + 2)
                V.tensor_scalar(meansq[:, half:half + 1], meansq[:, half:half + 1],
                                sumsq[:, 2 * half + 1:2 * half + 2], 1.0 / D, ALU.add, ALU.mult)\
                    .then_inc(pow_asked, 1)
                dve.wait_ge(pow_done, pow_no("norm", st, half))
                dve.wait_ge(gain_loaded, 16 * (st + 1))
                for b in range(2):
                    c = slice(b * HALFD, (b + 1) * HALFD)
                    dst = xn[:, c] if st < 4 else h[:, half, c]
                    V.scalar_tensor_tensor(dst, h[:, half, c], rstd[:, half:half + 1], gain[:, c],
                                           ALU.mult, ALU.mult).then_inc(normed, 1)

            def norm_lo(st, half):
                for b in range(2):
                    dve.wait_ge(xt_hi, 4 * st + 2 * half + b + 1)
                    hi = xT_hi[:, half, 4 * b:4 * b + 4, :].rearrange("p k t -> p (k t)")
                    lo = xT_lo[:, half, 4 * b:4 * b + 4, :].rearrange("p k t -> p (k t)")
                    V.tensor_tensor(lo, bank[:, 6 + b, :], hi.bitcast(F32), ALU.subtract).then_inc(xt_lo, 1)

            def k_evac(g):
                dve.wait_ge(slab_used, mix0[0] + NAT[0] + 2 * g + 2)
                for i in range(2):
                    r = slice(64 * i, 64 * i + 64)
                    last = V.tensor_copy(kT[r, i, :, :].rearrange("p s t -> p (s t)"), bank[r, 5, :])
                last.then_inc(k_copied, 1)

            def maxima(l, j):
                g, maps = 3 * l + j, 4 if l == 0 else 2
                scale = float(64 if l == 0 else 128) ** -0.5
                b0, *b1 = SCORE_BANKS[j]
                dve.wait_ge(scored, g + 1)
                V.reduce_max(rmax[:, 0:maps], bank[:, b0, 0:maps * P].rearrange("p (m k) -> p m k", m=maps), AX_X)
                if maps == 4:
                    V.reduce_max(rmax[:, 4:6], bank[:, b1[0], :].rearrange("p (m k) -> p m k", m=2), AX_X)
                    link(V.reduce_max(rmax[:, 6:8], bank[:, b1[1], :].rearrange("p (m k) -> p m k", m=2), AX_X))
                    V.tensor_scalar(nmax[:, :], rmax[:, :], -scale, None, ALU.mult).then_inc(nmax_ready, 1)
                else:
                    link(V.reduce_max(rmax[:, 4:6], bank[:, b1[0], :].rearrange("p (m k) -> p m k", m=2), AX_X))
                    both = rmax[:, :].rearrange("p (q m) -> p q m", q=2)[:, :, 0:2]
                    V.tensor_scalar(nmax[:, :].rearrange("p (q m) -> p q m", q=2)[:, :, 0:2], both,
                                    -scale, None, ALU.mult).then_inc(nmax_ready, 1)

            def combine(j):
                dve.wait_ge(exp_done, j + 1)
                link(V.reciprocal(rsum[:, :], sums[:, :]))
                link(V.tensor_tensor(rsum[:, :], rsum[:, :], coef[:, :], ALU.mult))
                for q, pq in ((0, p0), (1, p1)):
                    for hd in range(2):
                        last = V.tensor_scalar(pq[:, 2 * hd, :], pq[:, 2 * hd, :],
                                               rsum[:, 4 * q + 2 * hd:4 * q + 2 * hd + 1], None, ALU.mult)
                link(last)
                for q, pq in ((0, p0), (1, p1)):
                    for hd in range(2):
                        last = V.scalar_tensor_tensor(
                            pq[:, 2 * hd, :], pq[:, 2 * hd + 1, :],
                            rsum[:, 4 * q + 2 * hd + 1:4 * q + 2 * hd + 2], pq[:, 2 * hd, :], ALU.mult, ALU.add)
                last.then_inc(probs_ready, 1)

            def recips(j):
                dve.wait_ge(exp_done, 3 + j + 1)
                both = lambda t: t[:, :].rearrange("p (q m) -> p q m", q=2)[:, :, 0:2]
                V.reciprocal(both(rsum), both(sums)).then_inc(recip_ready, 1)

            def probT_evac(j):
                dve.wait_ge(prob_t, 2 * j + 2)
                V.tensor_copy(probT[:, 1, :, :].rearrange("p b q -> p (b q)"),
                              bank[:, PROB_T_BANKS[j][1], 0:3 * P]).then_inc(probT_b, 1)

            def o_norm(j):
                dve.wait_ge(o_squared, j + 1)
                V.tensor_scalar(osq[:, :], osq[:, :], 1.0 / HD, EPS, ALU.mult, ALU.add).then_inc(pow_asked, 1)
                dve.wait_ge(pow_done, pow_no("head", j))
                for i in range(4):
                    last = V.scalar_tensor_tensor(o_sb[:, i // 2, i % 2, :], bank[:, OUT_BANK[j], i * P:(i + 1) * P],
                                                  osq[:, i:i + 1], subg[:, :], ALU.mult, ALU.mult)
                last.then_inc(o_ready, 1)

            def y_lo_evac(l, j):
                dve.wait_ge(y_hi, 3 * l + j + 1)
                V.tensor_tensor(yT_lo[:, :, 2 + 2 * j:4 + 2 * j, :],
                                bank[:, Y_BANK[j], :].rearrange("p (h k t) -> p h k t", h=2, k=2),
                                yT_hi[:, :, 2 + 2 * j:4 + 2 * j, :].bitcast(F32), ALU.subtract).then_inc(y_lo, 1)

            def prepare():
                dve.wait_ge(params_loaded, 64)
                prod = lam_in[:, :, :].rearrange("p (a b) n -> p a b n", b=2)
                link(V.tensor_tensor(prod[:, :, 0, :], prod[:, :, 0, :], prod[:, :, 1, :], ALU.mult))
                V.reduce_sum(lam_t[:, 0:2], prod[:, :, 0, :], AX_X).then_inc(lam_exp, 1)
                link(V.memset(coef[:, :], 1.0))
                V.memset(kT[64:P, 0, :, :], 0.0)
                link(V.memset(kT[0:64, 1, :, :], 0.0))
                link(V.tensor_scalar(subg[:, :], subg[:, :], 1.0 - LAM_INIT, None, ALU.mult))
                link(V.tensor_scalar(chan_half[:, :, :], chan[:, :, TAPS + 1:TAPS + 3], 0.5, None, ALU.mult))

            def lambda_coef():
                dve.wait_ge(lam_exp, 2)
                link(V.tensor_scalar(lam_t[:, 0:1], lam_t[:, 3:4], lam_t[:, 2:3], -LAM_INIT,
                                     ALU.subtract, ALU.add))
                odd = coef[:, :].rearrange("p (a b) -> p a b", b=2)[:, :, 1]
                link(V.tensor_scalar(odd, odd, lam_t[:, 0:1], None, ALU.mult))

            def mix0_dve():
                prepare()
                split_los(4, 5, 6, 7)
                lambda_coef()
                k_evac(0)
                split_los(8)
                maxima(0, 0)
                split_los(9)
                combine(0)
                dve.wait_ge(branch_act, 4)
                for c in range(2):
                    last = V.scalar_tensor_tensor(
                        yT_lo[:, :, c, :], bank[:, 3, c * 256:(c + 1) * 256].rearrange("p (h t) -> p h t", h=2),
                        chan[:, c, TAPS + 3:TAPS + 4], yT_hi[:, :, c, :].bitcast(F32), ALU.mult, ALU.subtract)
                last.then_inc(branch_lo, 1)
                split_los(10)
                k_evac(1)
                probT_evac(0)
                split_los(11)
                o_norm(0)
                maxima(0, 1)
                split_los(12)
                combine(1)
                split_los(13)
                k_evac(2)
                y_lo_evac(0, 0)
                probT_evac(1)
                o_norm(1)
                maxima(0, 2)
                split_los(14)
                combine(2)
                y_lo_evac(0, 1)
                split_los(15)
                probT_evac(2)
                split_los(16)
                o_norm(2)
                y_lo_evac(0, 2)
                split_los(17)

            conv_n = [0]

            def conv(n):
                for _ in range(n):
                    k = conv_n[0]
                    if k >= 2 * TAPS:
                        return
                    tap, c = divmod(k, 2)
                    src = conv_in[:, c, tap:tap + SEQ]
                    w = chan[:, c, tap:tap + 1]
                    if tap == 0:
                        V.tensor_scalar(conv_acc[:, c, :], src, w, chan[:, c, TAPS:TAPS + 1], ALU.mult, ALU.add)\
                            .then_inc(conv_step, 1)
                    else:
                        dve.wait_ge(conv_step, k - 1)
                        V.scalar_tensor_tensor(conv_acc[:, c, :], src, w, conv_acc[:, c, :],
                                               ALU.mult, ALU.add).then_inc(conv_step, 1)
                    conv_n[0] += 1

            def mix1_dve():
                m, o, f = mix0[1], out0[1], ffn0[1]
                V.memset(conv_in[:, :, 0:PAD], 0.0).then_inc(branch_dve, 1)
                for half in range(HALVES):
                    dve.wait_ge(branch_act, 4 + half + 1)
                    V.scalar_tensor_tensor(tmp_a[:, half, :], tmp_t[:, half, :], 1.0, bank[:, 4, 0:256],
                                           ALU.add, ALU.mult).then_inc(branch_dve, 1)
                split_los(m + 6)
                dve.wait_ge(branch_act, 7)
                dve.wait_ge(branch_dve, 3)
                conv(20)
                split_los(m + 7, m + 8)
                conv(6)
                maxima(1, 0)
                split_los(m + 9)
                recips(0)
                conv(6)
                split_los(m + 10)
                conv(6)
                split_los(o)
                maxima(1, 1)
                conv(6)
                recips(1)
                split_los(o + 1)
                conv(10)
                y_lo_evac(1, 0)
                conv(6)
                split_los(o + 2)
                maxima(1, 2)
                split_los(o + 3)
                recips(2)
                conv(2 * TAPS)
                y_lo_evac(1, 1)
                split_los(f)
                split_los(f + 1)
                dve.wait_ge(branch_t, 5)
                for half in range(HALVES):
                    last = V.bn_stats(stats[:, half, :], bank[:, 7, half * 256:(half + 1) * 256])
                link(last)
                for half in range(HALVES):
                    last = V.bn_aggr(mv[:, half, :], stats[:, half, :])
                link(last)
                V.tensor_scalar(meansq[:, 2:4], mv[:, :, 1], EPS, None, ALU.add).then_inc(pow_asked, 1)
                y_lo_evac(1, 2)
                dve.wait_ge(pow_done, pow_no("ln", 0))
                for half in range(HALVES):
                    last = V.tensor_scalar(tmp_a[:, half, :], bank[:, 7, half * 256:(half + 1) * 256],
                                           mv[:, half, 0:1], rstd[:, 2 + half:3 + half], ALU.subtract, ALU.mult)
                last.then_inc(branch_dve, 1)
                split_los(f + 2)
                dve.wait_ge(branch_act, 9)
                for c in range(2):
                    last = V.tensor_scalar(conv_acc[:, c, :], bank[:, 4, c * 256:(c + 1) * 256],
                                           chan[:, c, TAPS + 1:TAPS + 2], chan[:, c, TAPS + 2:TAPS + 3],
                                           ALU.mult, ALU.add)
                link(last)
                V.scalar_tensor_tensor(conv_acc[:, :, :], conv_in[:, :, 0:SEQ], 1.0, conv_acc[:, :, :],
                                       ALU.add, ALU.mult).then_inc(branch_dve, 1)
                dve.wait_ge(branch_act, 10)
                dve.wait_ge(branch_dve, BR_CONV_W)
                for half in range(HALVES):
                    last = V.scalar_tensor_tensor(
                        yT_lo[:, half, 0:2, :], conv_acc[:, :, half * P:(half + 1) * P], 0.5,
                        yT_hi[:, half, 0:2, :].bitcast(F32), ALU.mult, ALU.subtract)
                last.then_inc(branch_lo, 1)
                split_los(f + 3)

            def ffn_dve(l):
                U = 22 * l

                def activate(n, p):
                    dve.wait_ge(tanh_done, U + n + 1)
                    V.scalar_tensor_tensor(tmp_a[:, p, :], tmp_t[:, p, :], 1.0, bank[:, 4 + p, 0:256],
                                           ALU.add, ALU.mult).then_inc(gated, 1)
                    dve.wait_ge(gated, U + n + 1)
                    V.scalar_tensor_tensor(tmp_a[:, p, :], tmp_a[:, p, :], 0.5, bank[:, 4 + p, 256:512],
                                           ALU.mult, ALU.mult).then_inc(act_ready, 1)

                def at_lo_evac(n, np_, ip, half):
                    dve.wait_ge(at_hi, U + n + 1)
                    hi = actT_hi[:, half, 2 * ip:2 * ip + 2, :].rearrange("p k t -> p (k t)")
                    lo = actT_lo[:, half, 2 * ip:2 * ip + 2, :].rearrange("p k t -> p (k t)")
                    V.tensor_tensor(lo, bank[:, 6 + np_, 0:256], hi.bitcast(F32), ALU.subtract).then_inc(at_lo, 1)

                f = ffn0[l]
                norm_add(2 * l + 1, 0)
                norm_scale(2 * l + 1, 0)
                norm_lo(2 * l + 1, 0)
                split_los(f + 4)
                norm_add(2 * l + 1, 1)
                norm_scale(2 * l + 1, 1)
                activate(0, 0)
                norm_lo(2 * l + 1, 1)
                split_los(f + 5)
                activate(1, 1)
                at_lo_evac(0, 0, 0, 0)
                activate(2, 0)
                split_los(f + 6, f + 7)
                at_lo_evac(1, 1, 1, 0)
                activate(3, 1)
                at_lo_evac(2, 0, 0, 1)

                def chunk(i, p):
                    s = up_slab(l, i) + 3
                    static = up_slab(l, 2 + p) + 3
                    split_lo(s, static)
                    activate(2 * i, 0)
                    at_lo_evac(2 * i - 1, 1, 1 - p, 1)
                    split_lo(s + 1, static + 1)
                    activate(2 * i + 1, 1)
                    at_lo_evac(2 * i, 0, p, 0)
                    split_lo(s + 2, static + 2)

                with dve.Fori(2, NCH - 1, 2) as i:
                    chunk(i, 0)
                    chunk(i + 1, 1)
                last = NCH - 1
                nxt = f + 3 * NCH
                split_los(nxt - 1)
                activate(2 * last, 0)
                at_lo_evac(2 * last - 1, 1, 1 - last % 2, 1)
                split_los(nxt)
                activate(2 * last + 1, 1)
                at_lo_evac(2 * last, 0, last % 2, 0)
                at_lo_evac(2 * last + 1, 1, last % 2, 1)
                split_los(nxt + 1)
                split_los(nxt + 2, nxt + 3)

            norm_scale(0, 0)
            split_los(0)
            norm_lo(0, 0)
            split_los(1)
            norm_scale(0, 1)
            split_los(2, 3)
            norm_lo(0, 1)
            mix0_dve()
            ffn_dve(0)
            norm_add(2, 0)
            norm_scale(2, 0)
            norm_lo(2, 0)
            split_los(mix0[1] + 4)
            norm_add(2, 1)
            norm_scale(2, 1)
            norm_lo(2, 1)
            split_los(mix0[1] + 5)
            mix1_dve()
            ffn_dve(1)
            for half in range(HALVES):
                norm_add(4, half)
                norm_scale(4, half)

        @block.tensor
        def _(pe):
            T = nc.tensor

            def split_product(o, st_hi, st_lo, mv_hi, mv_lo, first, last):
                T.matmul(o, st_hi, mv_lo, start=first, stop=False)
                T.matmul(o, st_hi, mv_hi, start=False, stop=False)
                return T.matmul(o, st_lo, mv_hi, start=False, stop=last)

            def w_part(s, c0, n):
                return w_hi[:, slot(s), c0:c0 + n], w_lo[:, slot(s), c0:c0 + n]

            def unit(s, static, half, b, width=512, slabs=2, release=False, done=None,
                     midway=None):
                per = KC // slabs
                for k in range(KC):
                    if k == KC // 2 and midway:
                        midway()
                    if k % per == 0:
                        pe.wait_ge(lo_ready, s + k // per + 1)
                    hi, lo = w_part(static + k // per, (k % per) * width, width)
                    last = split_product(bank[:, b, 0:width], xT_hi[:, half, k, :], xT_lo[:, half, k, :],
                                         hi, lo, k == 0, k == KC - 1)
                    if release and k % per == per - 1:
                        last.then_inc(slab_used, 1)
                if not release:
                    last.then_inc(done, 1)

            def norm_transposes(st, half):
                for b in range(2):
                    pe.wait_ge(normed, 4 * st + 2 * half + b + 1)
                    if half:
                        pe.wait_ge(xt_lo, 4 * st + b + 1)
                    for k in range(4):
                        last = T.transpose(bank[:, 6 + b, k * P:(k + 1) * P], xn[:, (4 * b + k) * P:(4 * b + k + 1) * P],
                                           ident[:, :])
                    last.then_inc(normed_t, 1)

            def x_ready(st, half):
                pe.wait_ge(xt_lo, 4 * st + 2 * half + 2)

            def qk_chunk(l, j):
                s = mix0[l] + NAT[l] + 2 * j
                pe.wait_ge(lo_ready, s + 2)
                for sub in range(4):
                    for k in range(KC):
                        hi, lo = w_part(s + k // 4, (k % 4) * 512 + sub * P, P)
                        last = split_product(bank[:, 4 + sub // 2, (sub % 2) * 256:(sub % 2) * 256 + 256],
                                             hi, lo, xT_hi[:, :, k, :], xT_lo[:, :, k, :], k == 0, k == KC - 1)
                        if sub == 3 and k % 4 == 3:
                            last.then_inc(slab_used, 1)
                    if sub == 1:
                        last.then_inc(q_done, 1)

            def scores(l, j):
                g, maps = 3 * l + j, 4 if l == 0 else 2
                b0, *b1 = SCORE_BANKS[j]
                pe.wait_ge(q_copied, g + 1)
                if l == 0:
                    pe.wait_ge(k_copied, j + 1)
                if g == 0:
                    pe.wait_ge(consts, 6)
                for m in range(maps):
                    sub, parity = divmod(m, 2) if l == 0 else (m, 0)
                    o = bank[:, b0, m * P:(m + 1) * P]
                    T.matmul(o, qT[:, sub, 0:P], kT[:, parity, sub, 0:P], start=True, stop=False)
                    T.matmul(o, ident_b[:, :], mask_b[:, :], start=False, stop=True)
                for m in range(maps):
                    sub, parity = divmod(m, 2) if l == 0 else (m, 0)
                    c = 256 * (m % 2)
                    T.matmul(bank[:, b1[m // 2], c:c + 256], qT[:, sub, P:2 * P], kT[:, parity, sub, :],
                             start=True, stop=False)
                    last = T.matmul(bank[:, b1[m // 2], c + P:c + 2 * P], ident_b[:, :], mask_b[:, :],
                                    start=False, stop=True)
                last.then_inc(scored, 1)

            def attend(l, j):
                g = 3 * l + j
                step = 2 if l == 0 else 1
                if l == 0:
                    pe.wait_ge(probs_ready, j + 1)
                else:
                    pe.wait_ge(exp_done, g + 1)
                if j:
                    pe.wait_ge(y_lo, g)
                for hd in range(2):
                    b = PROB_T_BANKS[j][hd]
                    m = step * hd
                    for i, src in enumerate((p0[:, m, :], p1[:, m, 0:P], p1[:, m, P:2 * P])):
                        last = T.transpose(bank[:, b, i * P:(i + 1) * P], src, ident[:, :])
                    last.then_inc(prob_t, 1)
                if g == 0:
                    pe.wait_ge(branch_lo, 1)
                for hd in range(2):
                    if l == 0:
                        pe.wait_ge((probT_a, probT_b)[hd], j + 1)
                    else:
                        pe.wait_ge(probT_a, 3 + 2 * j + hd + 1)
                    head = slice((2 * j + hd) * P, (2 * j + hd + 1) * P)
                    o = bank[:, OUT_BANK[j], hd * P:(hd + 1) * P]
                    T.matmul(o, probT[:, hd, 0, :], v[:, 0, head], start=True, stop=True)
                    o = bank[:, OUT_BANK[j], (2 + hd) * P:(3 + hd) * P]
                    T.matmul(o, probT[:, hd, 1, :], v[:, 0, head], start=True, stop=False)
                    last = T.matmul(o, probT[:, hd, 2, :], v[:, 1, head], start=False, stop=True)
                last.then_inc(o_done, 1)

            def y_transposes(l, j):
                pe.wait_ge(o_ready if l == 0 else o_scaled, j + 1)
                for i in range(4):
                    last = T.transpose(bank[:, Y_BANK[j], i * P:(i + 1) * P], o_sb[:, i // 2, i % 2, :], ident[:, :])
                last.then_inc(y_t, 1)

            def rows_product(s, static, half, act_hi, act_lo, first, last_slab, release):
                pe.wait_ge(lo_ready, s + 1)
                for b in range(2):
                    for k in range(2):
                        hi, lo = w_part(static, k * D + b * HALFD, HALFD)
                        last = split_product(bank[:, 2 * half + b, :], act_hi[:, k, :], act_lo[:, k, :],
                                             hi, lo, first and k == 0, last_slab and k == 1)
                    if last_slab and not (release and b):
                        last.then_inc(acc_done, 1)
                if release:
                    last.then_inc(slab_used, 1)

            def out_slab(l, o, half):
                k0 = OUT_ROWS[l][o]
                if k0:
                    pe.wait_ge(y_lo, 3 * l + k0 // 2)
                else:
                    pe.wait_ge(branch_lo, l + 1)
                rows_product(out0[l] + o, out0[l] + o, half, yT_hi[:, half, k0:k0 + 2, :],
                                    yT_lo[:, half, k0:k0 + 2, :], o == 0, o == 3, half == 1)

            def pool_differences():
                pe.wait_ge(consts, CONSTS_MADE)
                for g in range(4):
                    b, c = 6 + g // 2, 256 * (g % 2)
                    ch = slice(g * 64, (g + 1) * 64)
                    T.matmul(bank[0:64, b, c:c + 256], u_sb[:, 0, ch], branch[:, g, 0:256], start=True, stop=False)
                    last = T.matmul(bank[0:64, b, c + P:c + 2 * P], u_sb[:, 1, ch], branch[:, g, 256:384],
                                    start=False, stop=True)
                    if g % 2:
                        last.then_inc(branch_t, 1)

            def pool_map():
                pe.wait_ge(branch_act, 2)
                for g in range(4):
                    r = slice(64 * (g % 2), 64 * (g % 2) + 64)
                    c = 256 * (g // 2)
                    last = T.matmul(bank[r, 3, c:c + 256], pw_sb[:, g, :], dT[:, g, :], start=True, stop=True)
                last.then_inc(branch_t, 1)

            def mix(l):
                st, m = 2 * l, mix0[l]
                norm_transposes(st, 0)
                x_ready(st, 0)
                unit(m, m, 0, 4, done=nat_done)
                unit(m + 2, m + 2, 0, 5, done=nat_done, midway=lambda: norm_transposes(st, 1))
                x_ready(st, 1)
                n = 4 * l
                if l == 0:
                    pe.wait_ge(nat_copied, 1)
                else:
                    pe.wait_ge(branch_dve, 2)
                unit(m, m, 1, 4, release=True, done=nat_done)
                pe.wait_ge(nat_copied, 2 if l == 0 else 5)
                unit(m + 2, m + 2, 1, 5, release=True, done=nat_done)
                if l == 0:
                    pe.wait_ge(nat_copied, 4)
                else:
                    pe.wait_ge(branch_dve, 3)
                    for c in range(2):
                        for half in range(HALVES):
                            last = T.transpose(bank[:, 6, c * 256 + half * P:c * 256 + (half + 1) * P],
                                               tmp_a[:, half, c * P:(c + 1) * P], ident[:, :])
                    last.then_inc(branch_t, 1)
                    unit(m + 4, m + 4, 0, 4, 256, 1, done=nat_done)
                    pe.wait_ge(nat_copied, 6)
                    unit(m + 4, m + 4, 1, 5, 256, 1, release=True, done=nat_done)
                    pe.wait_ge(nat_copied, 8)
                g = 3 * l
                qk_chunk(l, 0)
                if l == 0:
                    pool_differences()
                scores(l, 0)
                if l == 0:
                    pool_map()
                qk_chunk(l, 1)
                attend(l, 0)
                scores(l, 1)
                qk_chunk(l, 2)
                y_transposes(l, 0)
                attend(l, 1)
                scores(l, 2)
                out_slab(l, 0, 0)
                out_slab(l, 0, 1)
                y_transposes(l, 1)
                out_slab(l, 1, 0)
                attend(l, 2)
                if l == 0:
                    out_slab(l, 2, 0)
                    out_slab(l, 1, 1)
                    y_transposes(l, 2)
                    out_slab(l, 3, 0)
                    out_slab(l, 2, 1)
                    out_slab(l, 3, 1)
                else:
                    pe.wait_ge(conv_step, 2 * TAPS)
                    for half in range(HALVES):
                        for c in range(2):
                            last = T.transpose(bank[:, 7, half * 256 + c * P:half * 256 + (c + 1) * P],
                                               conv_acc[:, c, half * P:(half + 1) * P], ident[:, :])
                    last.then_inc(branch_t, 1)
                    out_slab(l, 1, 1)
                    y_transposes(l, 2)
                    pe.wait_ge(branch_dve, 4)
                    for c in range(2):
                        for half in range(HALVES):
                            last = T.transpose(bank[:, 4, c * 256 + half * P:c * 256 + (half + 1) * P],
                                               tmp_a[:, half, c * P:(c + 1) * P], ident[:, :])
                    last.then_inc(branch_t, 1)
                    out_slab(l, 2, 0)
                    out_slab(l, 2, 1)
                    out_slab(l, 3, 0)
                    out_slab(l, 3, 1)

            def ffn(l):
                U, f = 22 * l, ffn0[l]

                def up(i, half, n, static, midway=None):
                    if in_register(n) or n >= 2:
                        pe.wait_ge(act_ready, U + n - 1)
                    unit(up_slab(l, i), static, half, 4 + (half if in_register(i) or i >= 2 else i),
                         release=half == 1, done=up_done, midway=midway)

                def transposes(n, p):
                    pe.wait_ge(act_ready, U + n + 1)
                    if in_register(n) or n >= 2:
                        pe.wait_ge(at_lo, U + n - 1)
                    for k in range(2):
                        last = T.transpose(bank[:, 6 + p, k * P:(k + 1) * P], tmp_a[:, p, k * P:(k + 1) * P],
                                           ident[:, :])
                    last.then_inc(act_t, 1)

                def down(i, n, static, half, ip, first=False, final=False):
                    pe.wait_ge(at_lo, U + n + 1)
                    rows_product(down_slab(l, i), static, half, actT_hi[:, half, 2 * ip:2 * ip + 2, :],
                                        actT_lo[:, half, 2 * ip:2 * ip + 2, :], first, final, half == 1)

                st = 2 * l + 1
                norm_transposes(st, 0)
                x_ready(st, 0)
                up(0, 0, 0, f)
                up(1, 0, 1, f + 2, midway=lambda: norm_transposes(st, 1))
                x_ready(st, 1)
                transposes(0, 0)
                up(0, 1, 2, f)
                transposes(1, 1)
                up(1, 1, 3, f + 2)
                transposes(2, 0)
                down(0, 0, f + 4, 0, 0, first=True)
                down(0, 2, f + 4, 1, 0, first=True)

                def chunk(i, p):
                    su, sd = up_slab(l, 2 + p), down_slab(l, 1 + p)
                    up(i, 0, 2 * i, su)
                    transposes(2 * i - 1, 1)
                    down(i - 1, 2 * i - 2 if in_register(i) else unit_no(i - 1, 0), sd, 0, 1 - p)
                    up(i, 1, 2 * i + 1, su)
                    transposes(2 * i, 0)
                    down(i - 1, 2 * i - 1, sd, 1, 1 - p)

                with pe.Fori(2, NCH - 1, 2) as i:
                    chunk(i, 0)
                    chunk(i + 1, 1)
                e = NCH - 1
                up(e, 0, 2 * e, up_slab(l, e))
                transposes(2 * e - 1, 1)
                up(e, 1, 2 * e + 1, up_slab(l, e))
                transposes(2 * e, 0)
                down(e - 1, 2 * e - 2, down_slab(l, e - 1), 0, (e - 1) % 2)
                transposes(2 * e + 1, 1)
                down(e, 2 * e, down_slab(l, e), 0, e % 2, final=True)
                down(e - 1, 2 * e - 1, down_slab(l, e - 1), 1, (e - 1) % 2)
                down(e, 2 * e + 1, down_slab(l, e), 1, e % 2, final=True)

            pe.wait_ge(consts, 3)
            for l in range(2):
                mix(l)
                ffn(l)


CONSTS_MADE = 6 + sum(1 + (w - 1) + 2 * 3 for w in POOL_WINDOWS)
BR_CONV_W = 5


_INS = ["x", "norm_mix_g", "norm_ffn_g", "norm_final_g", "ab_w_in", "ab_w_out", "pool_w", "diff_lambda",
        "diff_subln_g", "cd_w_in", "cd_w_out", "channel_params", "ffn_w_gate", "ffn_w_up", "ffn_w_down"]


def kernel(**inputs):
    import numpy as _np
    import concourse.bacc as _bacc
    from concourse import mybir as _mybir
    from concourse.bass_utils import run_bass_kernel_spmd as _run

    a = {k: _np.ascontiguousarray(t) for k, t in inputs.items()}
    a["x"] = a["x"][0]
    a["norm_final_g"] = a["norm_final_g"].reshape(1, -1)
    for k in ("ab_w_in", "ab_w_out", "pool_w", "diff_lambda", "cd_w_in", "cd_w_out"):
        a[k] = a[k][0]
    a["channel_params"] = _np.concatenate(
        [a["conv_w"][0].T] + [a[k][0][:, None] for k in ("conv_b", "conv_ln_g", "conv_ln_b", "pool_scale")], axis=1)
    nc = _bacc.Bacc("TRN2", target_bir_lowering=False, num_devices=1)
    arrays, args = {}, []
    for name in _INS:
        t = _np.ascontiguousarray(a[name])
        arrays[f"in_{name}"] = t
        args.append(nc.dram_tensor(f"in_{name}", t.shape, _mybir.dt.from_np(t.dtype), kind="ExternalInput").ap())
    args.append(nc.dram_tensor("out", a["x"].shape, _mybir.dt.float32, kind="ExternalOutput").ap())
    trunk(nc, *args)
    r = _run(nc, [arrays], core_ids=[0])
    return r.results[0]["out"].reshape(inputs["x"].shape)
```

```python
import math
from contextlib import ExitStack

import concourse.bass as bass
from concourse import mybir

F32 = mybir.dt.float32
F32R = mybir.dt.float32r
BF16 = mybir.dt.bfloat16
ALU = mybir.AluOpType
ACT = mybir.ActivationFunctionType
AX_X = mybir.AxisListType.X

P = 128
HALVES = 2
EPS = 1e-6
NEG = -1e30
POOL_WINDOWS = (2, 4, 8, 16)
LAM_INIT = 0.8 - 0.6 * math.exp(-0.3 * 0)

SLAB = 2048
RAW_SLOTS = 3
SLOTS = 6
LOADS = 2

SCORE_BANKS = ((0, 1, 2), (0, 1, 2), (6, 4, 5))
PROB_T_BANKS = ((6, 7), (6, 2), (7, 4))
OUT_BANK = ((3, 7, 5), (3, 7, 7))
Y_BANK = (3, 7, 6)


def trunk(nc, x, norm_mix_g, norm_ffn_g, norm_final_g, ab_w_in, ab_w_out, pool_w, diff_lambda,
          diff_subln_g, cd_w_in, cd_w_out, channel_params, ffn_w_gate, ffn_w_up, ffn_w_down, out):
    SEQ, D = x.shape
    KC = D // P
    POOL = pool_w.shape[1] * pool_w.shape[0]
    DFF = ffn_w_gate.shape[2]
    TAPS = channel_params.shape[1] - 4
    CONV = channel_params.shape[0]
    HEADS = 6
    HD = 128
    WIDTH = HEADS * HD
    NCH = DFF // 256
    HALFD = D // 2
    assert SEQ == 2 * P and D == 1024 and DFF % 256 == 0 and POOL == 256 and CONV == 256

    NAT = (4, 5)
    mix0 = [0, NAT[0] + 6 + 4 + 3 * NCH]
    out0 = [mix0[l] + NAT[l] + 6 for l in range(2)]
    ffn0 = [out0[l] + 4 for l in range(2)]
    SLABS = ffn0[1] + 3 * NCH

    OUT_ROWS = ((0, 2, 4, 6), (2, 4, 6, 0))

    def unit_no(i, half):
        return 2 * half + i if i < 2 else 2 * i + half

    def up_slab(l, i):
        return ffn0[l] + 2 * i if not in_register(i) and i < 2 else ffn0[l] + 3 * i - 1

    def down_slab(l, i):
        return ffn0[l] + 3 * i + (4 if in_register(i) or i < NCH - 1 else 2)

    def in_register(i):
        return not isinstance(i, int)

    ctx = ExitStack()
    with ctx:
        def sb(name, shape, dt=F32):
            return ctx.enter_context(nc.sbuf_tensor(name, shape, dt))

        def sem(name):
            return ctx.enter_context(nc.semaphore(name))

        raw = sb("raw", [P, RAW_SLOTS, SLAB])
        w_hi = sb("w_hi", [P, SLOTS, SLAB], F32R)
        w_lo = sb("w_lo", [P, SLOTS, SLAB], F32R)
        xT_hi = sb("xT_hi", [P, HALVES, KC, P], F32R)
        xT_lo = sb("xT_lo", [P, HALVES, KC, P], F32R)
        yT_hi = sb("yT_hi", [P, HALVES, KC, P], F32R)
        yT_lo = sb("yT_lo", [P, HALVES, KC, P], F32R)
        h = sb("h", [P, HALVES, D])
        xn = sb("xn", [P, D])
        gain = sb("gain", [P, D])
        v = sb("v", [P, HALVES, WIDTH])
        qT = sb("qT", [P, 2, SEQ])
        kT = sb("kT", [P, 2, 2, SEQ])
        work = sb("work", [P, 12, P])
        probT = sb("probT", [P, 2, 3, P])
        o_sb = sb("o_sb", [P, HALVES, 2, P])
        branch = sb("branch", [P, 4, 3 * P])
        u_sb = sb("u_sb", [P, HALVES, POOL])
        pw_sb = sb("pw_sb", [64, 4, 64])
        chan = sb("chan", [P, 2, TAPS + 4])
        chan_half = sb("chan_half", [P, 2, 2])
        subg = sb("subg", [P, HD])
        lam_in = sb("lam_in", [P, 4, 64])
        ident = sb("ident", [P, P])
        ident_b = sb("ident_b", [P, P], BF16)
        mask_b = sb("mask_b", [P, P], BF16)
        sumsq = sb("sumsq", [P, 4])
        power = sb("power", [P, 4])
        meansq = sb("meansq", [P, 4])
        rstd = sb("rstd", [P, 4])
        rmax = sb("rmax", [P, 8])
        nmax = sb("nmax", [P, 8])
        sums = sb("sums", [P, 8])
        coef = sb("coef", [P, 8])
        rsum = sb("rsum", [P, 8])
        osq = sb("osq", [P, 4])
        lam_t = sb("lam_t", [P, 4])
        stats = sb("stats", [P, HALVES, 6])
        mv = sb("mv", [P, HALVES, 2])
        bank = ctx.enter_context(nc.psum_tensor("bank", [P, 8, 512], F32))

        p0 = work[:, 0:4, :]
        p1 = work[:, 4:12, :].rearrange("p (m b) k -> p m (b k)", b=2)
        tmp_t = work[:, 0:4, :].rearrange("p (n b) k -> p n (b k)", b=2)
        tmp_a = work[:, 4:8, :].rearrange("p (n b) k -> p n (b k)", b=2)
        actT_hi = yT_hi[:, :, 0:4, :]
        actT_lo = yT_lo[:, :, 0:4, :]
        dT = xn[0:64, :].rearrange("p (g t) -> p g t", g=4)
        ln = xn[:, 0:HALFD].rearrange("p (n t) -> p n t", n=2)
        PAD = TAPS - 1
        conv_in = branch[:, 0:2, 0:PAD + SEQ]
        conv_acc = branch[:, 2:4, 0:SEQ]

        x_loaded = [sem(f"x_loaded{i}") for i in range(3)]
        gain_loaded = sem("gain_loaded")
        params_loaded = sem("params_loaded")
        out_stored = sem("out_stored")
        raw_loaded = [sem(f"raw_loaded{i}") for i in range(RAW_SLOTS)]
        first_loaded = sem("first_loaded")
        first_hi = sem("first_hi")
        first_lo = sem("first_lo")
        hi_ready = sem("hi_ready")
        lo_ready = sem("lo_ready")
        slab_used = sem("slab_used")
        consts = sem("consts")
        h_added = sem("h_added")
        squared = sem("squared")
        eps_added = sem("eps_added")
        pow_asked = sem("pow_asked")
        pow_done = sem("pow_done")
        normed = sem("normed")
        normed_t = sem("normed_t")
        xt_hi = sem("xt_hi")
        xt_lo = sem("xt_lo")
        nat_done = sem("nat_done")
        nat_copied = sem("nat_copied")
        q_done = sem("q_done")
        q_copied = sem("q_copied")
        k_copied = sem("k_copied")
        scored = sem("scored")
        nmax_ready = sem("nmax_ready")
        exp_done = sem("exp_done")
        probs_ready = sem("probs_ready")
        prob_t = sem("prob_t")
        probT_a = sem("probT_a")
        probT_b = sem("probT_b")
        o_done = sem("o_done")
        o_squared = sem("o_squared")
        o_ready = sem("o_ready")
        o_scaled = sem("o_scaled")
        recip_ready = sem("recip_ready")
        y_t = sem("y_t")
        y_hi = sem("y_hi")
        y_lo = sem("y_lo")
        branch_t = sem("branch_t")
        branch_act = sem("branch_act")
        branch_dve = sem("branch_dve")
        branch_lo = sem("branch_lo")
        conv_step = sem("conv_step")
        lam_exp = sem("lam_exp")
        up_done = sem("up_done")
        tanh_done = sem("tanh_done")
        gated = sem("gated")
        act_ready = sem("act_ready")
        act_t = sem("act_t")
        at_hi = sem("at_hi")
        at_lo = sem("at_lo")
        acc_done = sem("acc_done")
        dve_chain = sem("dve_chain")

        POWS = ([("norm", 0, 0), ("norm", 0, 1)] + [("head", j, 0) for j in range(3)]
                + [("norm", st, hf) for st in (1, 2) for hf in range(2)]
                + [("ln", 0, 0)] + [("norm", st, hf) for st in (3, 4) for hf in range(2)])

        def pow_no(kind, a, b=0):
            return POWS.index((kind, a, b)) + 1

        def slot(s):
            return s % SLOTS

        block = ctx.enter_context(nc.Block())

        @block.sync
        def _(sp):
            def into_slot(s):
                if in_register(s) or s >= RAW_SLOTS:
                    sp.wait_ge(lo_ready, s - RAW_SLOTS + 1)

            def load_columns(s, parts, k0, nk, static_slot):
                into_slot(s)
                width = sum(w for _, _, w in parts)
                dst = raw[:, static_slot % RAW_SLOTS, 0:nk * width].rearrange("p (k n) -> p k n", k=nk)
                at = 0
                for m, c0, w in parts:
                    src = m[k0 * P:(k0 + nk) * P, bass.ds(c0, w)].rearrange("(k p) n -> p k n", p=P)
                    sp.dma_start(dst[:, :, at:at + w], src).then_inc(raw_loaded[static_slot % RAW_SLOTS], 16)
                    at += w

            def load_rows(s, m, row0, static_slot):
                into_slot(s)
                for k in range(2):
                    sp.dma_start(raw[:, static_slot % RAW_SLOTS, k * D:(k + 1) * D],
                                 m[bass.ds(row0 + k * P, P), :]).then_inc(raw_loaded[static_slot % RAW_SLOTS], 16)

            def load_block(s, m, c0, w, k0, nk):
                into_slot(s)
                dst = raw[:, s % RAW_SLOTS, 0:nk * w].rearrange("p (k n) -> p k n", k=nk)
                for a, b, loaded in ((0, nk // 2, first_loaded), (nk // 2, nk * 3 // 4, None), (nk * 3 // 4, nk, None)) \
                        if s == 0 else ((0, nk // 2, None), (nk // 2, nk, None)):
                    src = m[(k0 + a) * P:(k0 + b) * P, c0:c0 + w].rearrange("(k p) n -> p k n", p=P)
                    sp.dma_start(dst[:, a:b, :], src).then_inc(loaded or raw_loaded[s % RAW_SLOTS], 16)

            def load_gain(st):
                g = [norm_mix_g[0:1, :], norm_ffn_g[0:1, :], norm_mix_g[1:2, :], norm_ffn_g[1:2, :],
                     norm_final_g][st]
                if st:
                    sp.wait_ge(normed, 4 * st)
                sp.dma_start(gain[:, :], g.broadcast_to([P, D]))\
                  .then_inc(gain_loaded, 16)

            def load_mix_in(l):
                w = (ab_w_in, cd_w_in)[l]
                s = mix0[l]
                c_v = POOL + 2 * WIDTH if l == 0 else 2 * CONV + 2 * WIDTH
                c_q = POOL if l == 0 else 2 * CONV
                c_k = c_q + WIDTH
                for k0 in (0, 4):
                    if l == 0:
                        load_block(s, w, c_v, 512, k0, 4)
                    else:
                        load_columns(s, [(w, 0, CONV), (w, CONV, CONV)], k0, 4, s)
                    s += 1
                for k0 in (0, 4):
                    if l == 0:
                        load_columns(s, [(w, 0, POOL), (w, c_v + 512, 256)], k0, 4, s)
                        if k0 == 0:
                            load_x(1)
                    else:
                        load_block(s, w, c_v, 512, k0, 4)
                    s += 1
                if l == 0:
                    load_params()
                else:
                    load_block(s, w, c_v + 512, 256, 0, 8)
                    s += 1
                for j in range(3):
                    for k0 in (0, 4):
                        load_columns(s, [(w, c_q + 256 * j, 256), (w, c_k + 256 * j, 256)], k0, 4, s)
                        s += 1

            def load_params():
                for dst, src in ((pw_sb[:, :, :], pool_w.rearrange("g c d -> c g d")),
                                 (chan[:, :, :], channel_params.rearrange("(c p) n -> p c n", p=P)),
                                 (subg[:, :], diff_subln_g.broadcast_to([P, HD])),
                                 (lam_in[:, :, :].rearrange("p a b -> p (a b)"),
                                  diff_lambda.rearrange("a b -> (a b)").rearrange("(o n) -> o n", o=1)
                                  .broadcast_to([P, 256]))):
                    sp.dma_start(dst, src).then_inc(params_loaded, 16)

            def load_ffn(l):
                def up(i, par):
                    s = up_slab(l, i)
                    for a in range(2):
                        load_columns(s + a, [(ffn_w_gate[l], i * 256, 256), (ffn_w_up[l], i * 256, 256)],
                                     4 * a, 4, par + a)

                def down(i, par):
                    load_rows(down_slab(l, i), ffn_w_down[l], i * 256, par)

                for i in range(2):
                    up(i, up_slab(l, i))
                down(0, down_slab(l, 0))
                with sp.Fori(2, NCH) as i:
                    up(i, up_slab(l, 2))
                    down(i - 1, down_slab(l, 1))
                down(NCH - 1, down_slab(l, NCH - 1))

            def load_x(half):
                for b in range(1 if half else 2):
                    c = slice(b * HALFD, D if half else (b + 1) * HALFD)
                    sp.dma_start(h[:, half, c], x[half * P:(half + 1) * P, c]).then_inc(x_loaded[2 * half + b], 16)

            load_x(0)
            load_gain(0)
            for l in range(2):
                load_mix_in(l)
                load_gain(2 * l + 1)
                for o in range(4):
                    load_rows(out0[l] + o, (ab_w_out, cd_w_out)[l], OUT_ROWS[l][o] * P, out0[l] + o)
                load_ffn(l)
                load_gain(2 * l + 2)
            for half in range(HALVES):
                for b in range(2):
                    c = slice(b * HALFD, (b + 1) * HALFD)
                    sp.wait_ge(normed, 16 + 2 * half + b + 1)
                    sp.dma_start(out[half * P:(half + 1) * P, c], h[:, half, c]).then_inc(out_stored, 16)
            sp.wait_ge(out_stored, 16 * 2 * HALVES)

        @block.gpsimd
        def _(pool):
            made = [0]

            def step(ins):
                made[0] += 1
                ins.then_inc(consts, 1)
                pool.wait_ge(consts, made[0])

            step(nc.gpsimd.memset(power[:, :], -0.5))
            step(nc.gpsimd.memset(ident[:, :], 0.0))
            step(nc.gpsimd.affine_select(out=ident[:, :], in_=ident[:, :], compare_op=ALU.not_equal, fill=1.0,
                                         base=0, pattern=[[-1, P]], channel_multiplier=1))
            IDENT_MADE = made[0]
            assert IDENT_MADE == 3
            for half in range(HALVES):
                pool.wait_ge(pow_asked, half + 1)
                nc.gpsimd.tensor_tensor(rstd[:, half:half + 1], meansq[:, half:half + 1],
                                        power[:, 0:1], ALU.pow).then_inc(pow_done, 1)
            step(nc.gpsimd.tensor_copy(ident_b[:, :], ident[:, :]))
            step(nc.gpsimd.memset(mask_b[:, :], 0.0))
            step(nc.gpsimd.affine_select(out=mask_b[:, :], in_=mask_b[:, :], compare_op=ALU.is_ge, fill=NEG,
                                         base=0, pattern=[[-1, P]], channel_multiplier=1))
            for g, w in enumerate(POOL_WINDOWS):
                step(nc.gpsimd.memset(branch[:, g, :], 1.0 / w))
                for t in range(w - 1):
                    step(nc.gpsimd.memset(branch[:, g, t:t + 1], 1.0 / (t + 1)))
                for c0, n in ((0, 2 * P), (2 * P, P)):
                    b = branch[:, g, c0:c0 + n]
                    step(nc.gpsimd.affine_select(out=b, in_=b, compare_op=ALU.is_ge, fill=0.0, base=0,
                                                 pattern=[[1, n]], channel_multiplier=-1))
                    step(nc.gpsimd.affine_select(out=b, in_=b, compare_op=ALU.is_ge, fill=0.0, base=w - 1,
                                                 pattern=[[-1, n]], channel_multiplier=1))
                    d = branch[:, g, c0:c0 + P]
                    step(nc.gpsimd.tensor_tensor(d, d, ident[:, :], ALU.subtract))
            assert made[0] == CONSTS_MADE
            for n, (kind, a, b) in enumerate(POWS):
                if n < 2:
                    continue
                pool.wait_ge(pow_asked, n + 1)
                if kind == "norm":
                    o, i, e = rstd[:, b:b + 1], meansq[:, b:b + 1], power[:, 0:1]
                elif kind == "head":
                    o, i, e = osq[:, :], osq[:, :], power[:, :]
                else:
                    o, i, e = rstd[:, 2:4], meansq[:, 2:4], power[:, 0:2]
                nc.gpsimd.tensor_tensor(o, i, e, ALU.pow).then_inc(pow_done, 1)

        @block.scalar
        def _(act):
            A = nc.scalar.activation

            def split_hi(s, static_slot=None, turn=None):
                t = s if static_slot is None else static_slot
                act.wait_ge(raw_loaded[t % RAW_SLOTS],
                            16 * LOADS * (s // RAW_SLOTS + 1) if turn is None else turn)
                if static_slot is not None or s >= SLOTS:
                    act.wait_ge(slab_used, s - SLOTS + 1)
                if static_slot is None and s == 0:
                    A(w_hi[:, 0, SLAB // 2:], raw[:, 0, SLAB // 2:], ACT.Copy).then_inc(hi_ready, 1)
                else:
                    A(w_hi[:, t % SLOTS, :], raw[:, t % RAW_SLOTS, :], ACT.Copy).then_inc(hi_ready, 1)

            def split_first_hi():
                act.wait_ge(first_loaded, 16)
                A(w_hi[:, 0, 0:SLAB // 2], raw[:, 0, 0:SLAB // 2], ACT.Copy).then_inc(first_hi, 1)

            def split_his(*slabs):
                for s in slabs:
                    if s < SLABS:
                        split_hi(s)

            def norm_squares(st, half):
                for b in range(2):
                    if st == 0:
                        if half == 0 or b == 0:
                            act.wait_ge(x_loaded[2 * half + b], 16)
                    else:
                        act.wait_ge(h_added, 4 * (st - 1) + 2 * half + b + 1)
                    if b == 1 or half == 1 or st > 0:
                        act.wait_ge(squared, 4 * st + 2 * half + b)
                    A(xn[:, b * HALFD:(b + 1) * HALFD], h[:, half, b * HALFD:(b + 1) * HALFD], ACT.Square,
                      accum_out=sumsq[:, 2 * half + b:2 * half + b + 1]).then_inc(squared, 1)

            def norm_hi(st, half, blocks=(0, 1)):
                for b in blocks:
                    act.wait_ge(normed_t, 4 * st + 2 * half + b + 1)
                    A(xT_hi[:, half, 4 * b:4 * b + 4, :].rearrange("p k t -> p (k t)"), bank[:, 6 + b, :],
                      ACT.Copy).then_inc(xt_hi, 1)

            def q_evac(g):
                l, j = divmod(g, 3)
                act.wait_ge(q_done, g + 1)
                last = A(qT[:, :, :].rearrange("p s t -> p (s t)"), bank[:, 4, :], ACT.Copy)
                if l == 1:
                    act.wait_ge(slab_used, mix0[l] + NAT[l] + 2 * j + 2)
                    last = A(kT[:, 0, :, :].rearrange("p s t -> p (s t)"), bank[:, 5, :], ACT.Copy)
                last.then_inc(q_copied, 1)

            def exps(l, j):
                g, maps = 3 * l + j, 4 if l == 0 else 2
                scale = float(64 if l == 0 else 128) ** -0.5
                b0, *b1 = SCORE_BANKS[j]
                act.wait_ge(nmax_ready, g + 1)
                for m in range(maps):
                    last = A(p0[:, m, :], bank[:, b0, m * P:(m + 1) * P], ACT.Exp, bias=nmax[:, m:m + 1],
                             scale=scale, accum_out=sums[:, m:m + 1])
                last.then_inc(exp_done, 1)
                for m in range(maps):
                    c = (m % 2) * 256
                    last = A(p1[:, m, :], bank[:, b1[m // 2], c:c + 256], ACT.Exp,
                             bias=nmax[:, 4 + m:5 + m], scale=scale, accum_out=sums[:, 4 + m:5 + m])
                last.then_inc(exp_done, 1)

            def probT_evac(l, j):
                g = 3 * l + j
                for hd in range(1 + l):
                    act.wait_ge(prob_t, 2 * g + hd + 1)
                    A(probT[:, hd, :, :].rearrange("p b q -> p (b q)"), bank[:, PROB_T_BANKS[j][hd], 0:3 * P],
                      ACT.Copy).then_inc(probT_a, 1)

            def o_scale(j):
                act.wait_ge(o_done, 3 + j + 1)
                act.wait_ge(recip_ready, j + 1)
                for i in range(4):
                    c = 4 * (i // 2) + i % 2
                    last = A(o_sb[:, i // 2, i % 2, :], bank[:, OUT_BANK[1][j], i * P:(i + 1) * P], ACT.Copy,
                             scale=rsum[:, c:c + 1])
                last.then_inc(o_scaled, 1)

            def o_squares(j):
                act.wait_ge(o_done, j + 1)
                for i in range(4):
                    last = A(o_sb[:, i // 2, i % 2, :], bank[:, OUT_BANK[0][j], i * P:(i + 1) * P], ACT.Square,
                             accum_out=osq[:, i:i + 1])
                last.then_inc(o_squared, 1)

            def y_hi_evac(l, j):
                act.wait_ge(y_t, 3 * l + j + 1)
                A(yT_hi[:, :, 2 + 2 * j:4 + 2 * j, :],
                  bank[:, Y_BANK[j], :].rearrange("p (h k t) -> p h k t", h=2, k=2), ACT.Copy).then_inc(y_hi, 1)

            def mix0_act():
                for half in range(HALVES):
                    act.wait_ge(*((nat_done, 1) if half == 0 else (slab_used, 2)))
                    A(v[:, half, 0:512], bank[:, 4, :], ACT.Copy).then_inc(nat_copied, 1)
                    act.wait_ge(*((nat_done, 2) if half == 0 else (slab_used, 4)))
                    A(u_sb[:, half, :], bank[:, 5, 0:POOL], ACT.Copy)
                    A(v[:, half, 512:768], bank[:, 5, 256:512], ACT.Copy).then_inc(nat_copied, 1)
                    if half == 0:
                        split_his(4, 5)
                act.wait_ge(lam_exp, 1)
                A(lam_t[:, 2:4], lam_t[:, 0:2], ACT.Exp).then_inc(lam_exp, 1)
                split_his(6, 7)
                q_evac(0)
                for i in range(2):
                    act.wait_ge(branch_t, i + 1)
                    A(dT[:, 2 * i:2 * i + 2, :].rearrange("p g t -> p (g t)"), bank[0:64, 6 + i, :], ACT.Copy)\
                        .then_inc(branch_act, 1)
                split_his(8, 9)
                exps(0, 0)
                act.wait_ge(branch_t, 3)
                for c in range(2):
                    A(yT_hi[:, :, c, :], bank[:, 3, c * 256:(c + 1) * 256].rearrange("p (h t) -> p h t", h=2),
                      ACT.Copy, scale=chan[:, c, TAPS + 3:TAPS + 4]).then_inc(branch_act, 1)
                split_his(10, 11)
                q_evac(1)
                probT_evac(0, 0)
                o_squares(0)
                split_his(12)
                exps(0, 1)
                split_his(13)
                q_evac(2)
                y_hi_evac(0, 0)
                probT_evac(0, 1)
                o_squares(1)
                y_hi_evac(0, 1)
                exps(0, 2)
                split_his(14)
                probT_evac(0, 2)
                o_squares(2)
                split_his(15)
                y_hi_evac(0, 2)
                split_his(16)

            def mix1_act():
                m, o, f = mix0[1], out0[1], ffn0[1]

                def gate_tanh(half):
                    act.wait_ge(*((nat_done, 3) if half == 0 else (slab_used, m + 2)))
                    A(tmp_t[:, half, :], bank[:, 4, 256:512], ACT.Tanh, scale=0.5).then_inc(branch_act, 1)

                def v_evac(half):
                    act.wait_ge(*((nat_done, 4) if half == 0 else (slab_used, m + 4)))
                    A(v[:, half, 0:512], bank[:, 5, :], ACT.Copy).then_inc(nat_copied, 1)

                def last_v_evac(half):
                    act.wait_ge(*((nat_done, 5) if half == 0 else (slab_used, m + 5)))
                    A(v[:, half, 512:768], bank[:, 4 + half, 0:256], ACT.Copy).then_inc(nat_copied, 1)

                gate_tanh(0)
                split_his(m + 4)
                norm_hi(2, 1)
                split_his(m + 5)
                v_evac(0)
                split_his(m + 6)
                gate_tanh(1)
                split_his(m + 7, m + 8)
                v_evac(1)
                act.wait_ge(branch_t, 4)
                A(conv_in[:, :, PAD:PAD + SEQ], bank[:, 6, :].rearrange("p (c t) -> p c t", c=2), ACT.Copy,
                  scale=0.5).then_inc(branch_act, 1)
                last_v_evac(0)
                split_his(m + 9)
                last_v_evac(1)
                split_his(m + 10)
                q_evac(3)
                exps(1, 0)
                split_his(o, o + 1)
                q_evac(4)
                probT_evac(1, 0)
                o_scale(0)
                exps(1, 1)
                split_his(o + 2, o + 3)
                q_evac(5)
                y_hi_evac(1, 0)
                probT_evac(1, 1)
                o_scale(1)
                split_his(f)
                exps(1, 2)
                y_hi_evac(1, 1)
                split_his(f + 1)
                probT_evac(1, 2)
                o_scale(2)
                act.wait_ge(branch_t, 6)
                for c in range(2):
                    A(conv_in[:, c, 0:SEQ], bank[:, 5, c * 256:(c + 1) * 256], ACT.Tanh,
                      bias=chan_half[:, c, 1:2], scale=chan_half[:, c, 0:1]).then_inc(branch_act, 1)
                y_hi_evac(1, 2)
                act.wait_ge(branch_dve, CONV_SWISHED)
                A(yT_hi[:, :, 0:2, :].rearrange("p h c t -> p c h t"),
                  conv_acc.rearrange("p c (h t) -> p c h t", h=2), ACT.Copy, scale=0.5).then_inc(branch_act, 1)
                split_his(f + 2)

            def ffn_act(l):
                U = 22 * l

                def tanh(i, half, p):
                    if half == 0:
                        act.wait_ge(up_done, NCH * l + i + 1)
                    else:
                        act.wait_ge(slab_used, up_slab(l, i) + 2)
                    A(tmp_t[:, p, :], bank[:, 4 + p, 0:256], ACT.Tanh, scale=0.5).then_inc(tanh_done, 1)

                def at_hi_evac(n, p, ip, half):
                    act.wait_ge(act_t, U + n + 1)
                    A(actT_hi[:, half, 2 * ip:2 * ip + 2, :].rearrange("p k t -> p (k t)"),
                      bank[:, 6 + p, 0:256], ACT.Copy).then_inc(at_hi, 1)

                f = ffn0[l]
                norm_squares(2 * l + 1, 0)
                norm_hi(2 * l + 1, 0)
                split_his(f + 3)
                norm_squares(2 * l + 1, 1)
                tanh(0, 0, 0)
                norm_hi(2 * l + 1, 1)
                split_his(f + 4)
                tanh(1, 0, 1)
                at_hi_evac(0, 0, 0, 0)
                split_his(f + 5)
                tanh(0, 1, 0)
                split_his(f + 6, f + 7)
                at_hi_evac(1, 1, 1, 0)
                tanh(1, 1, 1)
                at_hi_evac(2, 0, 0, 1)

                def chunk(i, p):
                    s, static = up_slab(l, i) + 3, up_slab(l, 2 + p) + 3

                    def split(a):
                        first = (static + a) // RAW_SLOTS + 1
                        split_hi(s + a, static + a, 16 * LOADS * (i + (first - 2 - p)))

                    split(0)
                    tanh(i, 0, 0)
                    at_hi_evac(2 * i - 1, 1, 1 - p, 1)
                    split(1)
                    tanh(i, 1, 1)
                    at_hi_evac(2 * i, 0, p, 0)
                    split(2)

                with act.Fori(2, NCH - 1, 2) as i:
                    chunk(i, 0)
                    chunk(i + 1, 1)
                last = NCH - 1
                nxt, st = f + 3 * NCH, 2 * l + 2
                split_his(nxt - 1)
                tanh(last, 0, 0)
                at_hi_evac(2 * last - 1, 1, 1 - last % 2, 1)
                split_his(nxt)
                at_hi_evac(2 * last, 0, last % 2, 0)
                split_his(nxt + 1)
                norm_squares(st, 0)
                split_his(nxt + 2)
                tanh(last, 1, 1)
                if l == 0:
                    norm_hi(st, 0, (0,))
                at_hi_evac(2 * last + 1, 1, last % 2, 1)
                if l == 0:
                    norm_hi(st, 0, (1,))
                split_his(nxt + 3)
                norm_squares(st, 1)

            norm_squares(0, 0)
            split_first_hi()
            norm_hi(0, 0)
            split_his(0, 1)
            norm_squares(0, 1)
            split_his(2)
            norm_hi(0, 1)
            split_his(3)
            mix0_act()
            ffn_act(0)
            mix1_act()
            ffn_act(1)

        @block.vector
        def _(dve):
            V = nc.vector
            chain = [0]

            def link(ins):
                chain[0] += 1
                ins.then_inc(dve_chain, 1)
                dve.wait_ge(dve_chain, chain[0])

            def split_lo(s, static=None):
                t = s if static is None else static
                dve.wait_ge(hi_ready, s + 1)
                c = slice(SLAB // 2 if static is None and s == 0 else 0, SLAB)
                V.tensor_tensor(w_lo[:, t % SLOTS, c], raw[:, t % RAW_SLOTS, c],
                                w_hi[:, t % SLOTS, c].bitcast(F32), ALU.subtract).then_inc(lo_ready, 1)

            def split_first_lo():
                dve.wait_ge(first_hi, 1)
                c = slice(0, SLAB // 2)
                V.tensor_tensor(w_lo[:, 0, c], raw[:, 0, c], w_hi[:, 0, c].bitcast(F32), ALU.subtract)\
                    .then_inc(first_lo, 1)

            def split_los(*slabs):
                for s in slabs:
                    if s < SLABS:
                        split_lo(s)

            def norm_add(st, half):
                for b in range(2):
                    if half and b:
                        dve.wait_ge(slab_used, (ffn0[0], mix0[1], ffn0[1], SLABS)[st - 1])
                    else:
                        dve.wait_ge(acc_done, 3 * (st - 1) + 2 * half + b + 1)
                    hp = h[:, half, b * HALFD:(b + 1) * HALFD]
                    V.tensor_tensor(hp, bank[:, 2 * half + b, :], hp, ALU.add).then_inc(h_added, 1)

            def norm_scale(st, half):
                n = 4 * st + 2 * half
                dve.wait_ge(squared, n + 1)
                link(V.tensor_scalar(meansq[:, half:half + 1], sumsq[:, 2 * half:2 * half + 1],
                                     D * EPS, None, ALU.add))
                dve.wait_ge(squared, n + 2)
                V.tensor_scalar(meansq[:, half:half + 1], meansq[:, half:half + 1],
                                sumsq[:, 2 * half + 1:2 * half + 2], 1.0 / D, ALU.add, ALU.mult)\
                    .then_inc(pow_asked, 1)
                dve.wait_ge(pow_done, pow_no("norm", st, half))
                dve.wait_ge(gain_loaded, 16 * (st + 1))
                for b in range(2):
                    c = slice(b * HALFD, (b + 1) * HALFD)
                    dst = xn[:, c] if st < 4 else h[:, half, c]
                    V.scalar_tensor_tensor(dst, h[:, half, c], rstd[:, half:half + 1], gain[:, c],
                                           ALU.mult, ALU.mult).then_inc(normed, 1)

            def norm_lo(st, half, blocks=(0, 1)):
                for b in blocks:
                    dve.wait_ge(xt_hi, 4 * st + 2 * half + b + 1)
                    hi = xT_hi[:, half, 4 * b:4 * b + 4, :].rearrange("p k t -> p (k t)")
                    lo = xT_lo[:, half, 4 * b:4 * b + 4, :].rearrange("p k t -> p (k t)")
                    V.tensor_tensor(lo, bank[:, 6 + b, :], hi.bitcast(F32), ALU.subtract).then_inc(xt_lo, 1)

            def k_evac(g):
                dve.wait_ge(slab_used, mix0[0] + NAT[0] + 2 * g + 2)
                for i in range(2):
                    r = slice(64 * i, 64 * i + 64)
                    last = V.tensor_copy(kT[r, i, :, :].rearrange("p s t -> p (s t)"), bank[r, 5, :])
                last.then_inc(k_copied, 1)

            def maxima(l, j):
                g, maps = 3 * l + j, 4 if l == 0 else 2
                scale = float(64 if l == 0 else 128) ** -0.5
                b0, *b1 = SCORE_BANKS[j]
                dve.wait_ge(scored, g + 1)
                V.reduce_max(rmax[:, 0:maps], bank[:, b0, 0:maps * P].rearrange("p (m k) -> p m k", m=maps), AX_X)
                if maps == 4:
                    V.reduce_max(rmax[:, 4:6], bank[:, b1[0], :].rearrange("p (m k) -> p m k", m=2), AX_X)
                    link(V.reduce_max(rmax[:, 6:8], bank[:, b1[1], :].rearrange("p (m k) -> p m k", m=2), AX_X))
                    V.tensor_scalar(nmax[:, :], rmax[:, :], -scale, None, ALU.mult).then_inc(nmax_ready, 1)
                else:
                    link(V.reduce_max(rmax[:, 4:6], bank[:, b1[0], :].rearrange("p (m k) -> p m k", m=2), AX_X))
                    both = rmax[:, :].rearrange("p (q m) -> p q m", q=2)[:, :, 0:2]
                    V.tensor_scalar(nmax[:, :].rearrange("p (q m) -> p q m", q=2)[:, :, 0:2], both,
                                    -scale, None, ALU.mult).then_inc(nmax_ready, 1)

            def combine(j):
                for q, pq in ((0, p0), (1, p1)):
                    dve.wait_ge(exp_done, 2 * j + q + 1)
                    c = slice(4 * q, 4 * q + 4)
                    link(V.reciprocal(rsum[:, c], sums[:, c]))
                    link(V.tensor_tensor(rsum[:, c], rsum[:, c], coef[:, c], ALU.mult))
                    for hd in range(2):
                        last = V.tensor_scalar(pq[:, 2 * hd, :], pq[:, 2 * hd, :],
                                               rsum[:, 4 * q + 2 * hd:4 * q + 2 * hd + 1], None, ALU.mult)
                    link(last)
                    for hd in range(2):
                        last = V.scalar_tensor_tensor(
                            pq[:, 2 * hd, :], pq[:, 2 * hd + 1, :],
                            rsum[:, 4 * q + 2 * hd + 1:4 * q + 2 * hd + 2], pq[:, 2 * hd, :], ALU.mult, ALU.add)
                last.then_inc(probs_ready, 1)

            def recips(j):
                dve.wait_ge(exp_done, 2 * (3 + j) + 2)
                both = lambda t: t[:, :].rearrange("p (q m) -> p q m", q=2)[:, :, 0:2]
                V.reciprocal(both(rsum), both(sums)).then_inc(recip_ready, 1)

            def probT_evac(j):
                dve.wait_ge(prob_t, 2 * j + 2)
                V.tensor_copy(probT[:, 1, :, :].rearrange("p b q -> p (b q)"),
                              bank[:, PROB_T_BANKS[j][1], 0:3 * P]).then_inc(probT_b, 1)

            def o_norm(j):
                dve.wait_ge(o_squared, j + 1)
                V.tensor_scalar(osq[:, :], osq[:, :], 1.0 / HD, EPS, ALU.mult, ALU.add).then_inc(pow_asked, 1)
                dve.wait_ge(pow_done, pow_no("head", j))
                for i in range(4):
                    last = V.scalar_tensor_tensor(o_sb[:, i // 2, i % 2, :], bank[:, OUT_BANK[0][j], i * P:(i + 1) * P],
                                                  osq[:, i:i + 1], subg[:, :], ALU.mult, ALU.mult)
                last.then_inc(o_ready, 1)

            def y_lo_evac(l, j):
                dve.wait_ge(y_hi, 3 * l + j + 1)
                V.tensor_tensor(yT_lo[:, :, 2 + 2 * j:4 + 2 * j, :],
                                bank[:, Y_BANK[j], :].rearrange("p (h k t) -> p h k t", h=2, k=2),
                                yT_hi[:, :, 2 + 2 * j:4 + 2 * j, :].bitcast(F32), ALU.subtract).then_inc(y_lo, 1)

            def prepare():
                dve.wait_ge(params_loaded, 64)
                prod = lam_in[:, :, :].rearrange("p (a b) n -> p a b n", b=2)
                link(V.tensor_tensor(prod[:, :, 0, :], prod[:, :, 0, :], prod[:, :, 1, :], ALU.mult))
                V.reduce_sum(lam_t[:, 0:2], prod[:, :, 0, :], AX_X).then_inc(lam_exp, 1)
                link(V.memset(coef[:, :], 1.0))
                V.memset(kT[64:P, 0, :, :], 0.0)
                link(V.memset(kT[0:64, 1, :, :], 0.0))
                link(V.tensor_scalar(subg[:, :], subg[:, :], 1.0 - LAM_INIT, None, ALU.mult))
                link(V.tensor_scalar(chan_half[:, :, :], chan[:, :, TAPS + 1:TAPS + 3], 0.5, None, ALU.mult))

            def lambda_coef():
                dve.wait_ge(lam_exp, 2)
                link(V.tensor_scalar(lam_t[:, 0:1], lam_t[:, 3:4], lam_t[:, 2:3], -LAM_INIT,
                                     ALU.subtract, ALU.add))
                odd = coef[:, :].rearrange("p (a b) -> p a b", b=2)[:, :, 1]
                link(V.tensor_scalar(odd, odd, lam_t[:, 0:1], None, ALU.mult))

            def mix0_dve():
                prepare()
                split_los(4, 5, 6, 7)
                lambda_coef()
                k_evac(0)
                split_los(8)
                maxima(0, 0)
                split_los(9)
                combine(0)
                dve.wait_ge(branch_act, 4)
                for c in range(2):
                    last = V.scalar_tensor_tensor(
                        yT_lo[:, :, c, :], bank[:, 3, c * 256:(c + 1) * 256].rearrange("p (h t) -> p h t", h=2),
                        chan[:, c, TAPS + 3:TAPS + 4], yT_hi[:, :, c, :].bitcast(F32), ALU.mult, ALU.subtract)
                last.then_inc(branch_lo, 1)
                split_los(10)
                k_evac(1)
                probT_evac(0)
                split_los(11)
                o_norm(0)
                maxima(0, 1)
                split_los(12)
                combine(1)
                split_los(13)
                k_evac(2)
                y_lo_evac(0, 0)
                probT_evac(1)
                o_norm(1)
                maxima(0, 2)
                y_lo_evac(0, 1)
                combine(2)
                probT_evac(2)
                split_los(14)
                o_norm(2)
                split_los(15)
                y_lo_evac(0, 2)

            conv_n = [0]

            def conv(n):
                for _ in range(n):
                    k = conv_n[0]
                    if k >= 2 * TAPS:
                        return
                    tap, c = divmod(k, 2)
                    src = conv_in[:, c, tap:tap + SEQ]
                    w = chan[:, c, tap:tap + 1]
                    if tap == 0:
                        V.tensor_scalar(conv_acc[:, c, :], src, w, chan[:, c, TAPS:TAPS + 1], ALU.mult, ALU.add)\
                            .then_inc(conv_step, 1)
                    else:
                        dve.wait_ge(conv_step, k - 1)
                        V.scalar_tensor_tensor(conv_acc[:, c, :], src, w, conv_acc[:, c, :],
                                               ALU.mult, ALU.add).then_inc(conv_step, 1)
                    conv_n[0] += 1

            def mix1_dve():
                m, o, f = mix0[1], out0[1], ffn0[1]

                def gated_branch(half):
                    dve.wait_ge(branch_act, 4 + half + 1)
                    V.scalar_tensor_tensor(tmp_a[:, half, :], tmp_t[:, half, :], 1.0, bank[:, 4, 0:256],
                                           ALU.add, ALU.mult).then_inc(branch_dve, 1)

                V.memset(conv_in[:, :, 0:PAD], 0.0).then_inc(branch_dve, 1)
                gated_branch(0)
                split_los(m + 4)
                norm_lo(2, 1)
                split_los(m + 5, m + 6)
                gated_branch(1)
                split_los(m + 7, m + 8)
                dve.wait_ge(branch_act, 7)
                dve.wait_ge(branch_dve, 3)
                conv(6)
                split_los(m + 9)
                conv(8)
                split_los(m + 10)
                conv(22)
                maxima(1, 0)
                split_los(o)
                recips(0)
                split_los(o + 1)
                conv(16)
                maxima(1, 1)
                split_los(o + 2)
                recips(1)
                split_los(o + 3)
                conv(2 * TAPS)
                y_lo_evac(1, 0)
                maxima(1, 2)
                dve.wait_ge(branch_t, 5)
                for half in range(HALVES):
                    last = V.bn_stats(stats[:, half, :], bank[:, 5, half * 256:(half + 1) * 256])
                link(last)
                for half in range(HALVES):
                    last = V.bn_aggr(mv[:, half, :], stats[:, half, :])
                link(last)
                V.tensor_scalar(meansq[:, 2:4], mv[:, :, 1], EPS, None, ALU.add).then_inc(pow_asked, 1)
                recips(2)
                dve.wait_ge(pow_done, pow_no("ln", 0))
                for half in range(HALVES):
                    last = V.tensor_scalar(ln[:, half, :], bank[:, 5, half * 256:(half + 1) * 256],
                                           mv[:, half, 0:1], rstd[:, 2 + half:3 + half], ALU.subtract, ALU.mult)
                last.then_inc(branch_dve, 1)
                y_lo_evac(1, 1)
                split_los(f, f + 1)
                dve.wait_ge(branch_act, 9)
                for c in range(2):
                    last = V.tensor_scalar(conv_acc[:, c, :], bank[:, 5, c * 256:(c + 1) * 256],
                                           chan[:, c, TAPS + 1:TAPS + 2], chan[:, c, TAPS + 2:TAPS + 3],
                                           ALU.mult, ALU.add)
                link(last)
                V.scalar_tensor_tensor(conv_acc[:, :, :], conv_in[:, :, 0:SEQ], 1.0, conv_acc[:, :, :],
                                       ALU.add, ALU.mult).then_inc(branch_dve, 1)
                y_lo_evac(1, 2)
                dve.wait_ge(branch_act, 10)
                dve.wait_ge(branch_dve, CONV_SWISHED)
                for half in range(HALVES):
                    last = V.scalar_tensor_tensor(
                        yT_lo[:, half, 0:2, :], conv_acc[:, :, half * P:(half + 1) * P], 0.5,
                        yT_hi[:, half, 0:2, :].bitcast(F32), ALU.mult, ALU.subtract)
                last.then_inc(branch_lo, 1)

            def ffn_dve(l):
                U = 22 * l

                def activate(n, p):
                    dve.wait_ge(tanh_done, U + n + 1)
                    V.scalar_tensor_tensor(tmp_a[:, p, :], tmp_t[:, p, :], 1.0, bank[:, 4 + p, 0:256],
                                           ALU.add, ALU.mult).then_inc(gated, 1)
                    dve.wait_ge(gated, U + n + 1)
                    V.scalar_tensor_tensor(tmp_a[:, p, :], tmp_a[:, p, :], 0.5, bank[:, 4 + p, 256:512],
                                           ALU.mult, ALU.mult).then_inc(act_ready, 1)

                def at_lo_evac(n, np_, ip, half):
                    dve.wait_ge(at_hi, U + n + 1)
                    hi = actT_hi[:, half, 2 * ip:2 * ip + 2, :].rearrange("p k t -> p (k t)")
                    lo = actT_lo[:, half, 2 * ip:2 * ip + 2, :].rearrange("p k t -> p (k t)")
                    V.tensor_tensor(lo, bank[:, 6 + np_, 0:256], hi.bitcast(F32), ALU.subtract).then_inc(at_lo, 1)

                f = ffn0[l]
                norm_add(2 * l + 1, 0)
                norm_scale(2 * l + 1, 0)
                norm_lo(2 * l + 1, 0)
                split_los(f + 2)
                norm_add(2 * l + 1, 1)
                norm_scale(2 * l + 1, 1)
                split_los(f + 3)
                activate(0, 0)
                norm_lo(2 * l + 1, 1)
                split_los(f + 4)
                activate(1, 1)
                at_lo_evac(0, 0, 0, 0)
                split_los(f + 5)
                activate(2, 0)
                split_los(f + 6, f + 7)
                at_lo_evac(1, 1, 1, 0)
                activate(3, 1)
                at_lo_evac(2, 0, 0, 1)

                def chunk(i, p):
                    s = up_slab(l, i) + 3
                    static = up_slab(l, 2 + p) + 3
                    split_lo(s, static)
                    activate(2 * i, 0)
                    at_lo_evac(2 * i - 1, 1, 1 - p, 1)
                    split_lo(s + 1, static + 1)
                    activate(2 * i + 1, 1)
                    at_lo_evac(2 * i, 0, p, 0)
                    split_lo(s + 2, static + 2)

                with dve.Fori(2, NCH - 1, 2) as i:
                    chunk(i, 0)
                    chunk(i + 1, 1)
                last = NCH - 1
                nxt, st = f + 3 * NCH, 2 * l + 2
                split_los(nxt - 1)
                activate(2 * last, 0)
                at_lo_evac(2 * last - 1, 1, 1 - last % 2, 1)
                at_lo_evac(2 * last, 0, last % 2, 0)
                split_los(nxt)
                norm_add(st, 0)
                norm_scale(st, 0)
                split_los(nxt + 1)
                activate(2 * last + 1, 1)
                if l == 0:
                    norm_lo(st, 0, (0,))
                at_lo_evac(2 * last + 1, 1, last % 2, 1)
                if l == 0:
                    norm_lo(st, 0, (1,))
                split_los(nxt + 2)
                norm_add(st, 1)
                norm_scale(st, 1)
                split_los(nxt + 3)

            norm_scale(0, 0)
            split_first_lo()
            norm_lo(0, 0)
            split_los(0, 1)
            norm_scale(0, 1)
            split_los(2)
            norm_lo(0, 1)
            split_los(3)
            mix0_dve()
            ffn_dve(0)
            mix1_dve()
            ffn_dve(1)

        @block.tensor
        def _(pe):
            T = nc.tensor

            def split_product(o, st_hi, st_lo, mv_hi, mv_lo, first, last):
                T.matmul(o, st_hi, mv_lo, start=first, stop=False)
                T.matmul(o, st_hi, mv_hi, start=False, stop=False)
                return T.matmul(o, st_lo, mv_hi, start=False, stop=last)

            def w_part(s, c0, n):
                return w_hi[:, slot(s), c0:c0 + n], w_lo[:, slot(s), c0:c0 + n]

            def unit(s, static, half, b, width=512, slabs=2, release=False, done=None, st=None,
                     midway=None):
                per = KC // slabs
                for k in range(KC):
                    if k == KC // 2 and midway:
                        midway()
                    if st is not None and k % 4 == 0:
                        pe.wait_ge(xt_lo, 4 * st + 2 * half + k // 4 + 1)
                    if st == 0 and half == 0 and k == 0:
                        pe.wait_ge(first_lo, 1)
                    elif st == 0 and half == 0 and k == 2:
                        pe.wait_ge(lo_ready, 1)
                    elif k % per == 0:
                        pe.wait_ge(lo_ready, s + k // per + 1)
                    hi, lo = w_part(static + k // per, (k % per) * width, width)
                    last = split_product(bank[:, b, 0:width], xT_hi[:, half, k, :], xT_lo[:, half, k, :],
                                         hi, lo, k == 0, k == KC - 1)
                    if release and k % per == per - 1:
                        last.then_inc(slab_used, 1)
                if not release:
                    last.then_inc(done, 1)

            def norm_transposes(st, half, blocks=(0, 1)):
                for b in blocks:
                    pe.wait_ge(normed, 4 * st + 2 * half + b + 1)
                    if half:
                        pe.wait_ge(xt_lo, 4 * st + b + 1)
                    for k in range(4):
                        last = T.transpose(bank[:, 6 + b, k * P:(k + 1) * P], xn[:, (4 * b + k) * P:(4 * b + k + 1) * P],
                                           ident[:, :])
                    last.then_inc(normed_t, 1)

            def qk_chunk(l, j):
                s = mix0[l] + NAT[l] + 2 * j
                pe.wait_ge(lo_ready, s + 2)
                for sub in range(4):
                    if j == 0 and sub % 2 == 0:
                        pe.wait_ge(nat_copied, (3, 7)[l] + sub // 2)
                    for k in range(KC):
                        hi, lo = w_part(s + k // 4, (k % 4) * 512 + sub * P, P)
                        last = split_product(bank[:, 4 + sub // 2, (sub % 2) * 256:(sub % 2) * 256 + 256],
                                             hi, lo, xT_hi[:, :, k, :], xT_lo[:, :, k, :], k == 0, k == KC - 1)
                        if sub == 3 and k % 4 == 3:
                            last.then_inc(slab_used, 1)
                    if sub == 1:
                        last.then_inc(q_done, 1)

            def scores(l, j):
                g, maps = 3 * l + j, 4 if l == 0 else 2
                b0, *b1 = SCORE_BANKS[j]
                pe.wait_ge(q_copied, g + 1)
                if l == 0:
                    pe.wait_ge(k_copied, j + 1)
                if g == 0:
                    pe.wait_ge(consts, 6)
                for m in range(maps):
                    sub, parity = divmod(m, 2) if l == 0 else (m, 0)
                    o = bank[:, b0, m * P:(m + 1) * P]
                    T.matmul(o, qT[:, sub, 0:P], kT[:, parity, sub, 0:P], start=True, stop=False)
                    T.matmul(o, ident_b[:, :], mask_b[:, :], start=False, stop=True)
                for m in range(maps):
                    sub, parity = divmod(m, 2) if l == 0 else (m, 0)
                    c = 256 * (m % 2)
                    T.matmul(bank[:, b1[m // 2], c:c + 256], qT[:, sub, P:2 * P], kT[:, parity, sub, :],
                             start=True, stop=False)
                    last = T.matmul(bank[:, b1[m // 2], c + P:c + 2 * P], ident_b[:, :], mask_b[:, :],
                                    start=False, stop=True)
                last.then_inc(scored, 1)

            def attend(l, j, between=None):
                g = 3 * l + j
                step = 2 if l == 0 else 1
                if l == 0:
                    pe.wait_ge(probs_ready, j + 1)
                else:
                    pe.wait_ge(exp_done, 2 * g + 2)
                if j == 2:
                    pe.wait_ge(y_lo, g)
                for hd in range(2):
                    b = PROB_T_BANKS[j][hd]
                    m = step * hd
                    for i, src in enumerate((p0[:, m, :], p1[:, m, 0:P], p1[:, m, P:2 * P])):
                        last = T.transpose(bank[:, b, i * P:(i + 1) * P], src, ident[:, :])
                    last.then_inc(prob_t, 1)
                if g == 0:
                    pe.wait_ge(branch_lo, 1)
                if between:
                    between()
                for hd in range(2):
                    if l == 0:
                        pe.wait_ge((probT_a, probT_b)[hd], j + 1)
                    else:
                        pe.wait_ge(probT_a, 3 + 2 * j + hd + 1)
                    head = slice((2 * j + hd) * P, (2 * j + hd + 1) * P)
                    o = bank[:, OUT_BANK[l][j], hd * P:(hd + 1) * P]
                    T.matmul(o, probT[:, hd, 0, :], v[:, 0, head], start=True, stop=True)
                    o = bank[:, OUT_BANK[l][j], (2 + hd) * P:(3 + hd) * P]
                    T.matmul(o, probT[:, hd, 1, :], v[:, 0, head], start=True, stop=False)
                    last = T.matmul(o, probT[:, hd, 2, :], v[:, 1, head], start=False, stop=True)
                last.then_inc(o_done, 1)

            def y_transposes(l, j):
                pe.wait_ge(o_ready if l == 0 else o_scaled, j + 1)
                for i in range(4):
                    last = T.transpose(bank[:, Y_BANK[j], i * P:(i + 1) * P], o_sb[:, i // 2, i % 2, :], ident[:, :])
                last.then_inc(y_t, 1)

            def rows_product(s, static, half, b, act_hi, act_lo, first, last_slab):
                pe.wait_ge(lo_ready, s + 1)
                for k in range(2):
                    hi, lo = w_part(static, k * D + b * HALFD, HALFD)
                    last = split_product(bank[:, 2 * half + b, :], act_hi[:, k, :], act_lo[:, k, :],
                                         hi, lo, first and k == 0, last_slab and k == 1)
                if half and b:
                    last.then_inc(slab_used, 1)
                elif last_slab:
                    last.then_inc(acc_done, 1)

            def out_slab(l, o, half, blocks=(0, 1)):
                k0 = OUT_ROWS[l][o]
                for b in blocks:
                    if k0:
                        pe.wait_ge(y_lo, 3 * l + k0 // 2)
                    else:
                        pe.wait_ge(branch_lo, l + 1)
                    if l == 0 and o == 0 and half and b:
                        pe.wait_ge(y_lo, 1)
                    rows_product(out0[l] + o, out0[l] + o, half, b, yT_hi[:, half, k0:k0 + 2, :],
                                 yT_lo[:, half, k0:k0 + 2, :], o == 0, o == 3)

            def pool_differences():
                pe.wait_ge(consts, CONSTS_MADE)
                for g in range(4):
                    b, c = 6 + g // 2, 256 * (g % 2)
                    ch = slice(g * 64, (g + 1) * 64)
                    T.matmul(bank[0:64, b, c:c + 256], u_sb[:, 0, ch], branch[:, g, 0:256], start=True, stop=False)
                    last = T.matmul(bank[0:64, b, c + P:c + 2 * P], u_sb[:, 1, ch], branch[:, g, 256:384],
                                    start=False, stop=True)
                    if g % 2:
                        last.then_inc(branch_t, 1)

            def pool_map():
                pe.wait_ge(branch_act, 2)
                for g in range(4):
                    r = slice(64 * (g % 2), 64 * (g % 2) + 64)
                    c = 256 * (g // 2)
                    last = T.matmul(bank[r, 3, c:c + 256], pw_sb[:, g, :], dT[:, g, :], start=True, stop=True)
                last.then_inc(branch_t, 1)

            def gated_transposes():
                pe.wait_ge(branch_dve, 3)
                for c in range(2):
                    for half in range(HALVES):
                        last = T.transpose(bank[:, 6, c * 256 + half * P:c * 256 + (half + 1) * P],
                                           tmp_a[:, half, c * P:(c + 1) * P], ident[:, :])
                last.then_inc(branch_t, 1)

            def conv_transposes():
                pe.wait_ge(conv_step, 2 * TAPS)
                for half in range(HALVES):
                    for c in range(2):
                        last = T.transpose(bank[:, 5, half * 256 + c * P:half * 256 + (c + 1) * P],
                                           conv_acc[:, c, half * P:(half + 1) * P], ident[:, :])
                last.then_inc(branch_t, 1)

            def layer_norm_transposes():
                pe.wait_ge(branch_dve, 4)
                for c in range(2):
                    for half in range(HALVES):
                        last = T.transpose(bank[:, 5, c * 256 + half * P:c * 256 + (half + 1) * P],
                                           ln[:, half, c * P:(c + 1) * P], ident[:, :])
                last.then_inc(branch_t, 1)

            def mix(l):
                st, m = 2 * l, mix0[l]
                unit(m, m, 0, 4, done=nat_done, st=st)
                unit(m + 2, m + 2, 0, 5, done=nat_done, midway=lambda: norm_transposes(st, 1))
                if l == 0:
                    pe.wait_ge(nat_copied, 1)
                else:
                    pe.wait_ge(branch_dve, 2)
                unit(m, m, 1, 4, release=True, st=st)
                pe.wait_ge(nat_copied, 2 if l == 0 else 5)
                unit(m + 2, m + 2, 1, 5, release=True)
                if l == 1:
                    gated_transposes()
                    unit(m + 4, m + 4, 0, 4, 256, 1, done=nat_done)
                    pe.wait_ge(nat_copied, 6)
                    unit(m + 4, m + 4, 1, 5, 256, 1, release=True)
                qk_chunk(l, 0)
                if l == 0:
                    pool_differences()
                scores(l, 0)
                if l == 0:
                    pool_map()
                qk_chunk(l, 1)
                attend(l, 0)
                scores(l, 1)
                qk_chunk(l, 2)
                y_transposes(l, 0)
                if l == 0:
                    attend(l, 1, lambda: out_slab(l, 0, 0, (0,)))
                    out_slab(l, 0, 0, (1,))
                    scores(l, 2)
                    y_transposes(l, 1)
                    out_slab(l, 0, 1)
                    out_slab(l, 1, 0)
                    out_slab(l, 1, 1)
                    attend(l, 2, lambda: out_slab(l, 2, 0, (0,)))
                    out_slab(l, 2, 0, (1,))
                    out_slab(l, 2, 1, (0,))
                    y_transposes(l, 2)
                    out_slab(l, 2, 1, (1,))
                    out_slab(l, 3, 0)
                    out_slab(l, 3, 1)
                    norm_transposes(st + 1, 0)
                else:
                    attend(l, 1)
                    scores(l, 2)
                    conv_transposes()
                    out_slab(l, 0, 0)
                    y_transposes(l, 1)
                    out_slab(l, 0, 1)
                    attend(l, 2, lambda: out_slab(l, 1, 0, (0,)))
                    out_slab(l, 1, 0, (1,))
                    layer_norm_transposes()
                    out_slab(l, 1, 1, (0,))
                    y_transposes(l, 2)
                    out_slab(l, 1, 1, (1,))
                    out_slab(l, 2, 0)
                    out_slab(l, 3, 0)
                    out_slab(l, 2, 1)
                    out_slab(l, 3, 1, (0,))
                    norm_transposes(st + 1, 0, (0,))
                    out_slab(l, 3, 1, (1,))
                    norm_transposes(st + 1, 0, (1,))

            def ffn(l):
                U, f = 22 * l, ffn0[l]

                def up(i, half, n, static, st=None, midway=None):
                    if in_register(n) or n >= 2:
                        pe.wait_ge(act_ready, U + n - 1)
                    unit(up_slab(l, i), static, half, 4 + (half if in_register(i) or i >= 2 else i),
                         release=half == 1, done=up_done, st=st, midway=midway)

                def transposes(n, p):
                    pe.wait_ge(act_ready, U + n + 1)
                    if in_register(n) or n >= 2:
                        pe.wait_ge(at_lo, U + n - 1)
                    for k in range(2):
                        last = T.transpose(bank[:, 6 + p, k * P:(k + 1) * P], tmp_a[:, p, k * P:(k + 1) * P],
                                           ident[:, :])
                    last.then_inc(act_t, 1)

                def down(i, n, static, half, ip, first=False, final=False, between=None):
                    pe.wait_ge(at_lo, U + n + 1)
                    for b in range(2):
                        rows_product(down_slab(l, i), static, half, b, actT_hi[:, half, 2 * ip:2 * ip + 2, :],
                                     actT_lo[:, half, 2 * ip:2 * ip + 2, :], first, final)
                        if b == 0 and between:
                            between()

                st = 2 * l + 1
                up(0, 0, 0, f, st=st)
                up(1, 0, 1, f + 2, midway=lambda: norm_transposes(st, 1))
                pe.wait_ge(xt_lo, 4 * st + 3)
                transposes(0, 0)
                up(0, 1, 2, f, st=st)
                transposes(1, 1)
                up(1, 1, 3, f + 2)
                transposes(2, 0)
                down(0, 0, f + 4, 0, 0, first=True)
                down(0, 2, f + 4, 1, 0, first=True)

                def chunk(i, p):
                    su, sd = up_slab(l, 2 + p), down_slab(l, 1 + p)
                    up(i, 0, 2 * i, su)
                    transposes(2 * i - 1, 1)
                    down(i - 1, 2 * i - 2 if in_register(i) else unit_no(i - 1, 0), sd, 0, 1 - p)
                    up(i, 1, 2 * i + 1, su)
                    transposes(2 * i, 0)
                    down(i - 1, 2 * i - 1, sd, 1, 1 - p)

                with pe.Fori(2, NCH - 1, 2) as i:
                    chunk(i, 0)
                    chunk(i + 1, 1)
                e = NCH - 1
                up(e, 0, 2 * e, up_slab(l, e))
                transposes(2 * e - 1, 1)
                down(e - 1, 2 * e - 2, down_slab(l, e - 1), 0, (e - 1) % 2, between=lambda: transposes(2 * e, 0))
                down(e, 2 * e, down_slab(l, e), 0, e % 2, final=True)
                up(e, 1, 2 * e + 1, up_slab(l, e))
                if l == 0:
                    norm_transposes(st + 1, 0, (0,))
                down(e - 1, 2 * e - 1, down_slab(l, e - 1), 1, (e - 1) % 2, between=lambda: transposes(2 * e + 1, 1))
                pe.wait_ge(at_lo, U + 2 * e + 2)
                if l == 0:
                    norm_transposes(st + 1, 0, (1,))
                down(e, 2 * e + 1, down_slab(l, e), 1, e % 2, final=True)

            pe.wait_ge(consts, 3)
            norm_transposes(0, 0)
            for l in range(2):
                mix(l)
                ffn(l)


CONV_SWISHED = 5
CONSTS_MADE = 6 + sum(1 + (w - 1) + 2 * 3 for w in POOL_WINDOWS)


_INS = ["x", "norm_mix_g", "norm_ffn_g", "norm_final_g", "ab_w_in", "ab_w_out", "pool_w", "diff_lambda",
        "diff_subln_g", "cd_w_in", "cd_w_out", "channel_params", "ffn_w_gate", "ffn_w_up", "ffn_w_down"]


def kernel(**inputs):
    import numpy as _np
    import concourse.bacc as _bacc
    from concourse import mybir as _mybir
    from concourse.bass_utils import run_bass_kernel_spmd as _run

    a = {k: _np.ascontiguousarray(t) for k, t in inputs.items()}
    a["x"] = a["x"][0]
    a["norm_final_g"] = a["norm_final_g"].reshape(1, -1)
    for k in ("ab_w_in", "ab_w_out", "pool_w", "diff_lambda", "cd_w_in", "cd_w_out"):
        a[k] = a[k][0]
    a["channel_params"] = _np.concatenate(
        [a["conv_w"][0].T] + [a[k][0][:, None] for k in ("conv_b", "conv_ln_g", "conv_ln_b", "pool_scale")], axis=1)
    nc = _bacc.Bacc("TRN2", target_bir_lowering=False, num_devices=1)
    arrays, args = {}, []
    for name in _INS:
        t = _np.ascontiguousarray(a[name])
        arrays[f"in_{name}"] = t
        args.append(nc.dram_tensor(f"in_{name}", t.shape, _mybir.dt.from_np(t.dtype), kind="ExternalInput").ap())
    args.append(nc.dram_tensor("out", a["x"].shape, _mybir.dt.float32, kind="ExternalOutput").ap())
    trunk(nc, *args)
    r = _run(nc, [arrays], core_ids=[0])
    return r.results[0]["out"].reshape(inputs["x"].shape)
```

```python
import math
from contextlib import ExitStack

import concourse.bass as bass
from concourse import mybir

F32 = mybir.dt.float32
F32R = mybir.dt.float32r
BF16 = mybir.dt.bfloat16
ALU = mybir.AluOpType
ACT = mybir.ActivationFunctionType
AX_X = mybir.AxisListType.X

P = 128
HALVES = 2
EPS = 1e-6
NEG = -1e30
POOL_WINDOWS = (2, 4, 8, 16)
LAM_INIT = 0.8 - 0.6 * math.exp(-0.3 * 0)

IDENT_MADE = 4
MASK_MADE = IDENT_MADE + 3
CONSTS_MADE = MASK_MADE + sum(1 + (w - 1) + 2 * 3 for w in POOL_WINDOWS)
CONV_SWISHED = 5

SLAB = 2048
PARTED = 4
RAW_SLOTS = 3
SLOTS = 6
LOADS = 2

SCORE_BANKS = ((0, 1, 2), (0, 1, 2), (6, 4, 5))
PROB_T_BANKS = ((6, 7), (6, 2), (7, 4))
POOL_BANK = 1
OUT_BANK = (3, 7, 5)
Y_BANK = ((3, 7, 6), (3, 7, 7))


def trunk(nc, x, norm_mix_g, norm_ffn_g, norm_final_g, ab_w_in, ab_w_out, pool_w, diff_lambda,
          diff_subln_g, cd_w_in, cd_w_out, channel_params, ffn_w_gate, ffn_w_up, ffn_w_down, out):
    SEQ, D = x.shape
    KC = D // P
    POOL = pool_w.shape[1] * pool_w.shape[0]
    DFF = ffn_w_gate.shape[2]
    TAPS = channel_params.shape[1] - 4
    CONV = channel_params.shape[0]
    HEADS = 6
    HD = 128
    WIDTH = HEADS * HD
    NCH = DFF // 256
    HALFD = D // 2
    assert SEQ == 2 * P and D == 1024 and DFF % 256 == 0 and POOL == 256 and CONV == 256

    NAT = (4, 5)
    mix0 = [0, NAT[0] + 6 + 4 + 3 * NCH]
    out0 = [mix0[l] + NAT[l] + 6 for l in range(2)]
    ffn0 = [out0[l] + 4 for l in range(2)]
    SLABS = ffn0[1] + 3 * NCH

    OUT_ROWS = ((2, 4, 0, 6), (2, 4, 6, 0))

    def in_register(i):
        return not isinstance(i, int)

    def unit_no(i, half):
        return 2 * half + i if i < 2 else 2 * i + half

    def up_slab(l, i):
        return ffn0[l] + 2 * i if not in_register(i) and i < 2 else ffn0[l] + 3 * i - 1

    def down_slab(l, i):
        return ffn0[l] + 3 * i + (4 if in_register(i) or i < NCH - 1 else 2)

    ctx = ExitStack()
    with ctx:
        def sb(name, shape, dt=F32):
            return ctx.enter_context(nc.sbuf_tensor(name, shape, dt))

        def sem(name):
            return ctx.enter_context(nc.semaphore(name))

        raw = sb("raw", [P, RAW_SLOTS, SLAB])
        w_hi = sb("w_hi", [P, SLOTS, SLAB], F32R)
        w_lo = sb("w_lo", [P, SLOTS, SLAB], F32R)
        xT_hi = sb("xT_hi", [P, HALVES, KC, P], F32R)
        xT_lo = sb("xT_lo", [P, HALVES, KC, P], F32R)
        yT_hi = sb("yT_hi", [P, HALVES, KC, P], F32R)
        yT_lo = sb("yT_lo", [P, HALVES, KC, P], F32R)
        h = sb("h", [P, HALVES, D])
        xn = sb("xn", [P, D])
        gain = sb("gain", [P, D])
        v = sb("v", [P, HALVES, WIDTH])
        qT = sb("qT", [P, 2, SEQ])
        kT = sb("kT", [P, 2, 2, SEQ])
        work = sb("work", [P, 12, P])
        probT = sb("probT", [P, 2, 3, P])
        o_sb = sb("o_sb", [P, HALVES, 2, P])
        branch = sb("branch", [P, 4, 3 * P])
        u_sb = sb("u_sb", [P, HALVES, POOL])
        pw_sb = sb("pw_sb", [64, 4, 64])
        chan = sb("chan", [P, 2, TAPS + 4])
        chan_half = sb("chan_half", [P, 2, 2])
        subg = sb("subg", [P, HD])
        lam_in = sb("lam_in", [P, 4, 64])
        ident = sb("ident", [P, P])
        ident_b = sb("ident_b", [P, P], BF16)
        mask_b = sb("mask_b", [P, 4, P], BF16)
        sumsq = sb("sumsq", [P, 4])
        ones = sb("ones", [1, P])
        power = sb("power", [P, 4])
        meansq = sb("meansq", [P, 4])
        rstd = sb("rstd", [P, 4])
        rmax = sb("rmax", [P, 8])
        nmax = sb("nmax", [P, 8])
        sums = sb("sums", [P, 8])
        coef = sb("coef", [P, 8])
        rsum = sb("rsum", [P, 8])
        osq = sb("osq", [P, 4])
        lam_t = sb("lam_t", [P, 4])
        stats = sb("stats", [P, HALVES, 6])
        mv = sb("mv", [P, HALVES, 2])
        bank = ctx.enter_context(nc.psum_tensor("bank", [P, 8, 512], F32))

        p0 = work[:, 0:4, :]
        p1 = work[:, 4:12, :].rearrange("p (m b) k -> p m (b k)", b=2)
        tmp_t = work[:, 0:4, :].rearrange("p (n b) k -> p n (b k)", b=2)
        tmp_a = work[:, 4:8, :].rearrange("p (n b) k -> p n (b k)", b=2)
        actT_hi = yT_hi[:, :, 0:4, :]
        actT_lo = yT_lo[:, :, 0:4, :]
        dT = xn[0:64, :].rearrange("p (g t) -> p g t", g=4)
        gained = kT[:, :, :, :].rearrange("p m s t -> p m (s t)")
        ln = xn[:, 0:HALFD].rearrange("p (n t) -> p n t", n=2)
        PAD = TAPS - 1
        conv_in = branch[:, 0:2, 0:PAD + SEQ]
        conv_acc = branch[:, 2:4, 0:SEQ]

        x_loaded = [sem(f"x_loaded{i}") for i in range(3)]
        gain_loaded = sem("gain_loaded")
        params_loaded = sem("params_loaded")
        out_stored = sem("out_stored")
        raw_loaded = [sem(f"raw_loaded{i}") for i in range(RAW_SLOTS)]
        first_loaded = sem("first_loaded")
        hi_ready = sem("hi_ready")
        lo_ready = sem("lo_ready")
        slab_used = sem("slab_used")
        part_hi = sem("part_hi")
        part_lo = sem("part_lo")
        consts = sem("consts")
        acc_done = sem("acc_done")
        h_added = sem("h_added")
        squared = sem("squared")
        pow_asked = sem("pow_asked")
        pow_done = sem("pow_done")
        gain_spread = sem("gain_spread")
        normed = sem("normed")
        gain_used = sem("gain_used")
        last_scaled = sem("last_scaled")
        normed_t = sem("normed_t")
        xt_hi = sem("xt_hi")
        xt_lo = sem("xt_lo")
        nat_done = sem("nat_done")
        nat_copied = sem("nat_copied")
        q_done = sem("q_done")
        q_copied = sem("q_copied")
        k_copied = sem("k_copied")
        scored = sem("scored")
        nmax_ready = sem("nmax_ready")
        exp_done = sem("exp_done")
        probs_ready = sem("probs_ready")
        prob_t = sem("prob_t")
        probT_a = sem("probT_a")
        probT_b = sem("probT_b")
        o_done = sem("o_done")
        o_squared = sem("o_squared")
        o_ready = sem("o_ready")
        y_t = sem("y_t")
        y_hi = sem("y_hi")
        y_lo = sem("y_lo")
        lam_exp = sem("lam_exp")
        branch_t = sem("branch_t")
        branch_act = sem("branch_act")
        branch_dve = sem("branch_dve")
        branch_lo = sem("branch_lo")
        conv_step = sem("conv_step")
        up_done = sem("up_done")
        tanh_done = sem("tanh_done")
        gated = sem("gated")
        act_ready = sem("act_ready")
        act_t = sem("act_t")
        at_hi = sem("at_hi")
        at_lo = sem("at_lo")
        dve_chain = sem("dve_chain")

        POWS = ([("norm", 0, 0), ("norm", 0, 1)] + [("head", j, 0) for j in range(3)]
                + [("norm", st, hf) for st in (1, 2) for hf in range(2)]
                + [("ln", 0, 0)] + [("norm", st, hf) for st in (3, 4) for hf in range(2)])

        def pow_no(kind, a, b=0):
            return POWS.index((kind, a, b)) + 1

        def slot(s):
            return s % SLOTS

        block = ctx.enter_context(nc.Block())

        @block.sync
        def _(sp):
            def into_slot(s):
                if in_register(s) or s >= RAW_SLOTS:
                    sp.wait_ge(lo_ready, s - RAW_SLOTS + 1)

            def load_columns(s, parts, k0, nk, static_slot):
                into_slot(s)
                width = sum(w for _, _, w in parts)
                dst = raw[:, static_slot % RAW_SLOTS, 0:nk * width].rearrange("p (k n) -> p k n", k=nk)
                at = 0
                for m, c0, w in parts:
                    src = m[k0 * P:(k0 + nk) * P, bass.ds(c0, w)].rearrange("(k p) n -> p k n", p=P)
                    sp.dma_start(dst[:, :, at:at + w], src).then_inc(raw_loaded[static_slot % RAW_SLOTS], 16)
                    at += w

            def load_rows(s, m, row0, static_slot):
                into_slot(s)
                for k in range(2):
                    sp.dma_start(raw[:, static_slot % RAW_SLOTS, k * D:(k + 1) * D],
                                 m[bass.ds(row0 + k * P, P), :]).then_inc(raw_loaded[static_slot % RAW_SLOTS], 16)

            def load_block(s, m, c0, w, k0, nk):
                into_slot(s)
                dst = raw[:, s % RAW_SLOTS, 0:nk * w].rearrange("p (k n) -> p k n", k=nk)
                for a, b, loaded in ((0, nk // 2, first_loaded), (nk // 2, nk * 3 // 4, None), (nk * 3 // 4, nk, None)) \
                        if s == 0 else ((0, nk // 2, None), (nk // 2, nk, None)):
                    src = m[(k0 + a) * P:(k0 + b) * P, c0:c0 + w].rearrange("(k p) n -> p k n", p=P)
                    sp.dma_start(dst[:, a:b, :], src).then_inc(loaded or raw_loaded[s % RAW_SLOTS], 16)

            def load_gain(st):
                g = [norm_ffn_g[0:1, :], norm_mix_g[1:2, :], norm_ffn_g[1:2, :], norm_final_g][st - 1]
                sp.wait_ge(normed, 4 * st)
                sp.dma_start(gain[:, :], g.broadcast_to([P, D])).then_inc(gain_loaded, 16)

            def load_mix_in(l):
                w = (ab_w_in, cd_w_in)[l]
                s = mix0[l]
                c_v = POOL + 2 * WIDTH if l == 0 else 2 * CONV + 2 * WIDTH
                c_q = POOL if l == 0 else 2 * CONV
                c_k = c_q + WIDTH
                for k0 in (0, 4):
                    if l == 0:
                        load_block(s, w, c_v, 512, k0, 4)
                    else:
                        load_columns(s, [(w, 0, CONV), (w, CONV, CONV)], k0, 4, s)
                    s += 1
                for k0 in (0, 4):
                    if l == 0:
                        load_columns(s, [(w, 0, POOL), (w, c_v + 512, 256)], k0, 4, s)
                        if k0 == 0:
                            load_x(1)
                    else:
                        load_block(s, w, c_v, 512, k0, 4)
                    s += 1
                if l == 0:
                    load_params()
                else:
                    load_block(s, w, c_v + 512, 256, 0, 8)
                    s += 1
                for j in range(3):
                    for k0 in (0, 4):
                        load_columns(s, [(w, c_q + 256 * j, 256), (w, c_k + 256 * j, 256)], k0, 4, s)
                        s += 1

            def load_params():
                for dst, src in ((pw_sb[:, :, :], pool_w.rearrange("g c d -> c g d")),
                                 (chan[:, :, :], channel_params.rearrange("(c p) n -> p c n", p=P)),
                                 (subg[:, :], diff_subln_g.broadcast_to([P, HD])),
                                 (lam_in[:, :, :].rearrange("p a b -> p (a b)"),
                                  diff_lambda.rearrange("a b -> (a b)").rearrange("(o n) -> o n", o=1)
                                  .broadcast_to([P, 256]))):
                    sp.dma_start(dst, src).then_inc(params_loaded, 16)

            def load_ffn(l):
                def up(i, par):
                    s = up_slab(l, i)
                    for a in range(2):
                        load_columns(s + a, [(ffn_w_gate[l], i * 256, 256), (ffn_w_up[l], i * 256, 256)],
                                     4 * a, 4, par + a)

                def down(i, par):
                    load_rows(down_slab(l, i), ffn_w_down[l], i * 256, par)

                for i in range(2):
                    up(i, up_slab(l, i))
                down(0, down_slab(l, 0))
                with sp.Fori(2, NCH) as i:
                    up(i, up_slab(l, 2))
                    down(i - 1, down_slab(l, 1))
                down(NCH - 1, down_slab(l, NCH - 1))

            def load_x(half):
                for b in range(1 if half else 2):
                    c = slice(b * HALFD, D if half else (b + 1) * HALFD)
                    sp.dma_start(h[:, half, c], x[half * P:(half + 1) * P, c]).then_inc(x_loaded[2 * half + b], 16)

            load_x(0)
            for l in range(2):
                load_mix_in(l)
                load_gain(2 * l + 1)
                for o in range(4):
                    load_rows(out0[l] + o, (ab_w_out, cd_w_out)[l], OUT_ROWS[l][o] * P, out0[l] + o)
                load_ffn(l)
                load_gain(2 * l + 2)
            for half in range(HALVES):
                for b in range(2):
                    c = slice(b * HALFD, (b + 1) * HALFD)
                    sp.wait_ge((normed, last_scaled)[b], (17 + half, 1 + half)[b])
                    sp.dma_start(out[half * P:(half + 1) * P, c], h[:, half, c]).then_inc(out_stored, 16)
            sp.wait_ge(out_stored, 16 * 2 * HALVES)

        @block.gpsimd
        def _(pool):
            made = [0]

            def step(ins):
                made[0] += 1
                ins.then_inc(consts, 1)
                pool.wait_ge(consts, made[0])

            step(nc.gpsimd.memset(ones[:, :], 1.0))
            step(nc.gpsimd.memset(power[:, :], -0.5))
            step(nc.gpsimd.memset(ident[:, :], 0.0))
            step(nc.gpsimd.affine_select(out=ident[:, :], in_=ident[:, :], compare_op=ALU.not_equal, fill=1.0,
                                         base=0, pattern=[[-1, P]], channel_multiplier=1))
            assert made[0] == IDENT_MADE
            for half in range(HALVES):
                pool.wait_ge(pow_asked, half + 1)
                nc.gpsimd.tensor_tensor(rstd[:, half:half + 1], meansq[:, half:half + 1],
                                        power[:, 0:1], ALU.pow).then_inc(pow_done, 1)
            step(nc.gpsimd.tensor_copy(ident_b[:, :], ident[:, :]))
            step(nc.gpsimd.memset(mask_b[:, :, :], 0.0))
            step(nc.gpsimd.affine_select(out=mask_b[:, :, :], in_=mask_b[:, :, :], compare_op=ALU.is_ge, fill=NEG,
                                         base=0, pattern=[[0, 4], [-1, P]], channel_multiplier=1))
            for g, w in enumerate(POOL_WINDOWS):
                step(nc.gpsimd.memset(branch[:, g, :], 1.0 / w))
                for t in range(w - 1):
                    step(nc.gpsimd.memset(branch[:, g, t:t + 1], 1.0 / (t + 1)))
                for c0, n in ((0, 2 * P), (2 * P, P)):
                    b = branch[:, g, c0:c0 + n]
                    step(nc.gpsimd.affine_select(out=b, in_=b, compare_op=ALU.is_ge, fill=0.0, base=0,
                                                 pattern=[[1, n]], channel_multiplier=-1))
                    step(nc.gpsimd.affine_select(out=b, in_=b, compare_op=ALU.is_ge, fill=0.0, base=w - 1,
                                                 pattern=[[-1, n]], channel_multiplier=1))
                    d = branch[:, g, c0:c0 + P]
                    step(nc.gpsimd.tensor_tensor(d, d, ident[:, :], ALU.subtract))
            assert made[0] == CONSTS_MADE
            for n, (kind, a, b) in enumerate(POWS):
                if n < 2:
                    continue
                pool.wait_ge(pow_asked, n + 1)
                if kind == "norm":
                    o, i, e = rstd[:, b:b + 1], meansq[:, b:b + 1], power[:, 0:1]
                elif kind == "head":
                    o, i, e = osq[:, :], osq[:, :], power[:, :]
                else:
                    o, i, e = rstd[:, 2:4], meansq[:, 2:4], power[:, 0:2]
                nc.gpsimd.tensor_tensor(o, i, e, ALU.pow).then_inc(pow_done, 1)

        @block.scalar
        def _(act):
            A = nc.scalar.activation

            def split_hi(s, static_slot=None, turn=None):
                t = s if static_slot is None else static_slot
                act.wait_ge(raw_loaded[t % RAW_SLOTS],
                            16 * LOADS * (s // RAW_SLOTS + 1) if turn is None else turn)
                if static_slot is not None or s >= SLOTS:
                    act.wait_ge(slab_used, s - SLOTS + 1)
                if static_slot is None and s < PARTED:
                    if s:
                        part_his(s)
                    c = slice(SLAB // 2, SLAB)
                    A(w_hi[:, s, c], raw[:, s % RAW_SLOTS, c], ACT.Copy).then_inc(hi_ready, 1)
                else:
                    A(w_hi[:, t % SLOTS, :], raw[:, t % RAW_SLOTS, :], ACT.Copy).then_inc(hi_ready, 1)

            def part_his(s):
                if s == 0:
                    act.wait_ge(first_loaded, 16)
                c = slice(0, SLAB // 2)
                A(w_hi[:, s, c], raw[:, s % RAW_SLOTS, c], ACT.Copy).then_inc(part_hi, 1)

            def split_his(*slabs):
                for s in slabs:
                    if s < SLABS:
                        split_hi(s)

            def norm_squares(st, half):
                for b in range(2):
                    if st == 0:
                        if half == 0 or b == 0:
                            act.wait_ge(x_loaded[2 * half + b], 16)
                    else:
                        act.wait_ge(h_added, 4 * (st - 1) + 2 * half + b + 1)
                    if b == 1 or half == 1 or st > 0:
                        act.wait_ge(squared, 4 * st + 2 * half + b)
                    A(xn[:, b * HALFD:(b + 1) * HALFD], h[:, half, b * HALFD:(b + 1) * HALFD], ACT.Square,
                      accum_out=sumsq[:, 2 * half + b:2 * half + b + 1]).then_inc(squared, 1)

            def norm_hi(st, half, blocks=(0, 1)):
                for b in blocks:
                    act.wait_ge(normed_t, 4 * st + 2 * half + b + 1)
                    A(xT_hi[:, half, 4 * b:4 * b + 4, :].rearrange("p k t -> p (k t)"), bank[:, 6 + b, :],
                      ACT.Copy).then_inc(xt_hi, 1)

            def q_evac(g):
                l, j = divmod(g, 3)
                act.wait_ge(q_done, g + 1)
                last = A(qT[:, :, :].rearrange("p s t -> p (s t)"), bank[:, 4, :], ACT.Copy)
                if l == 1:
                    act.wait_ge(slab_used, mix0[l] + NAT[l] + 2 * j + 2)
                    last = A(kT[:, 0, :, :].rearrange("p s t -> p (s t)"), bank[:, 5, :], ACT.Copy)
                last.then_inc(q_copied, 1)

            def exps(l, j):
                g, maps = 3 * l + j, 4 if l == 0 else 2
                scale = float(64 if l == 0 else 128) ** -0.5
                b0, *b1 = SCORE_BANKS[j]
                act.wait_ge(nmax_ready, 2 * g + 1)
                for m in range(maps):
                    last = A(p0[:, m, :], bank[:, b0, m * P:(m + 1) * P], ACT.Exp, bias=nmax[:, m:m + 1],
                             scale=scale, accum_out=sums[:, m:m + 1])
                last.then_inc(exp_done, 1)
                act.wait_ge(nmax_ready, 2 * g + 2)
                for m in range(maps):
                    c = (m % 2) * 256
                    last = A(p1[:, m, :], bank[:, b1[m // 2], c:c + 256], ACT.Exp,
                             bias=nmax[:, 4 + m:5 + m], scale=scale, accum_out=sums[:, 4 + m:5 + m])
                last.then_inc(exp_done, 1)

            def probT_evac(l, j):
                g = 3 * l + j
                for hd in range(1 + l):
                    act.wait_ge(prob_t, 2 * g + hd + 1)
                    A(probT[:, hd, :, :].rearrange("p b q -> p (b q)"), bank[:, PROB_T_BANKS[j][hd], 0:3 * P],
                      ACT.Copy).then_inc(probT_a, 1)

            def o_squares(j):
                act.wait_ge(o_done, j + 1)
                for i in range(4):
                    last = A(o_sb[:, i // 2, i % 2, :], bank[:, OUT_BANK[j], i * P:(i + 1) * P], ACT.Square,
                             accum_out=osq[:, i:i + 1])
                last.then_inc(o_squared, 1)

            def y_hi_evac(l, j):
                act.wait_ge(y_t, 3 * l + j + 1)
                A(yT_hi[:, :, 2 + 2 * j:4 + 2 * j, :],
                  bank[:, Y_BANK[l][j], :].rearrange("p (h k t) -> p h k t", h=2, k=2), ACT.Copy).then_inc(y_hi, 1)

            def mix0_act():
                for half in range(HALVES):
                    act.wait_ge(*((nat_done, 1) if half == 0 else (slab_used, 2)))
                    A(v[:, half, 0:512], bank[:, 4, :], ACT.Copy).then_inc(nat_copied, 1)
                    act.wait_ge(*((nat_done, 2) if half == 0 else (slab_used, 4)))
                    A(u_sb[:, half, :], bank[:, 5, 0:POOL], ACT.Copy)
                    A(v[:, half, 512:768], bank[:, 5, 256:512], ACT.Copy).then_inc(nat_copied, 1)
                    if half == 0:
                        split_his(4, 5)
                act.wait_ge(lam_exp, 1)
                A(lam_t[:, 2:4], lam_t[:, 0:2], ACT.Exp).then_inc(lam_exp, 1)
                split_his(6, 7)
                q_evac(0)
                for i in range(2):
                    act.wait_ge(branch_t, i + 1)
                    A(dT[:, 2 * i:2 * i + 2, :].rearrange("p g t -> p (g t)"), bank[0:64, 6 + i, :], ACT.Copy)\
                        .then_inc(branch_act, 1)
                split_his(8, 9)
                exps(0, 0)
                split_his(10, 11)
                q_evac(1)
                probT_evac(0, 0)
                o_squares(0)
                split_his(12)
                exps(0, 1)
                split_his(13)
                q_evac(2)
                y_hi_evac(0, 0)
                probT_evac(0, 1)
                act.wait_ge(branch_t, 3)
                for c in range(2):
                    A(yT_hi[:, :, c, :], bank[:, POOL_BANK, c * 256:(c + 1) * 256].rearrange("p (h t) -> p h t", h=2),
                      ACT.Copy, scale=chan[:, c, TAPS + 3:TAPS + 4]).then_inc(branch_act, 1)
                o_squares(1)
                y_hi_evac(0, 1)
                exps(0, 2)
                split_his(14)
                probT_evac(0, 2)
                o_squares(2)
                split_his(15)
                y_hi_evac(0, 2)
                split_his(16)

            def mix1_act():
                m, o, f = mix0[1], out0[1], ffn0[1]

                def gate_tanh(half):
                    act.wait_ge(*((nat_done, 3) if half == 0 else (slab_used, m + 2)))
                    A(tmp_t[:, half, :], bank[:, 4, 256:512], ACT.Tanh, scale=0.5).then_inc(branch_act, 1)

                def v_evac(half):
                    act.wait_ge(*((nat_done, 4) if half == 0 else (slab_used, m + 4)))
                    A(v[:, half, 0:512], bank[:, 5, :], ACT.Copy).then_inc(nat_copied, 1)

                def last_v_evac(half):
                    act.wait_ge(*((nat_done, 5) if half == 0 else (slab_used, m + 5)))
                    A(v[:, half, 512:768], bank[:, 4 + half, 0:256], ACT.Copy).then_inc(nat_copied, 1)

                gate_tanh(0)
                split_his(m + 4)
                norm_hi(2, 1)
                split_his(m + 5)
                v_evac(0)
                split_his(m + 6)
                gate_tanh(1)
                split_his(m + 7, m + 8)
                v_evac(1)
                act.wait_ge(branch_t, 4)
                A(conv_in[:, :, PAD:PAD + SEQ], bank[:, 6, :].rearrange("p (c t) -> p c t", c=2), ACT.Copy,
                  scale=0.5).then_inc(branch_act, 1)
                last_v_evac(0)
                split_his(m + 9)
                last_v_evac(1)
                split_his(m + 10)
                q_evac(3)
                split_his(o)
                exps(1, 0)
                split_his(o + 1)
                q_evac(4)
                probT_evac(1, 0)
                y_hi_evac(1, 0)
                exps(1, 1)
                split_his(o + 2, o + 3)
                q_evac(5)
                probT_evac(1, 1)
                y_hi_evac(1, 1)
                exps(1, 2)
                split_his(f)
                probT_evac(1, 2)
                split_his(f + 1)
                y_hi_evac(1, 2)
                act.wait_ge(branch_t, 6)
                for c in range(2):
                    A(conv_in[:, c, 0:SEQ], bank[:, 5, c * 256:(c + 1) * 256], ACT.Tanh,
                      bias=chan_half[:, c, 1:2], scale=chan_half[:, c, 0:1]).then_inc(branch_act, 1)
                act.wait_ge(branch_dve, CONV_SWISHED)
                A(yT_hi[:, :, 0:2, :].rearrange("p h c t -> p c h t"),
                  conv_acc.rearrange("p c (h t) -> p c h t", h=2), ACT.Copy, scale=0.5).then_inc(branch_act, 1)
                split_his(f + 2)

            def last_scale(half):
                act.wait_ge(pow_done, pow_no("norm", 4, half))
                act.wait_ge(gain_used, 2 * half + 2)
                A(h[:, half, HALFD:], gained[:, 1, :], ACT.Copy, scale=rstd[:, half:half + 1])\
                    .then_inc(last_scaled, 1)

            def ffn_act(l):
                U = 2 * NCH * l

                def tanh(i, half, p):
                    if half == 0:
                        act.wait_ge(up_done, NCH * l + i + 1)
                    else:
                        act.wait_ge(slab_used, up_slab(l, i) + 2)
                    A(tmp_t[:, p, :], bank[:, 4 + p, 0:256], ACT.Tanh, scale=0.5).then_inc(tanh_done, 1)

                def at_hi_evac(n, p, ip, half):
                    act.wait_ge(act_t, U + n + 1)
                    A(actT_hi[:, half, 2 * ip:2 * ip + 2, :].rearrange("p k t -> p (k t)"),
                      bank[:, 6 + p, 0:256], ACT.Copy).then_inc(at_hi, 1)

                f = ffn0[l]
                norm_squares(2 * l + 1, 0)
                norm_hi(2 * l + 1, 0)
                split_his(f + 3)
                norm_squares(2 * l + 1, 1)
                tanh(0, 0, 0)
                norm_hi(2 * l + 1, 1)
                split_his(f + 4)
                tanh(1, 0, 1)
                at_hi_evac(0, 0, 0, 0)
                split_his(f + 5)
                tanh(0, 1, 0)
                split_his(f + 6, f + 7)
                at_hi_evac(1, 1, 1, 0)
                tanh(1, 1, 1)
                at_hi_evac(2, 0, 0, 1)

                def chunk(i, p):
                    s, static = up_slab(l, i) + 3, up_slab(l, 2 + p) + 3

                    def split(a):
                        first = (static + a) // RAW_SLOTS + 1
                        split_hi(s + a, static + a, 16 * LOADS * (i + (first - 2 - p)))

                    split(0)
                    tanh(i, 0, 0)
                    at_hi_evac(2 * i - 1, 1, 1 - p, 1)
                    split(1)
                    tanh(i, 1, 1)
                    at_hi_evac(2 * i, 0, p, 0)
                    split(2)

                with act.Fori(2, NCH - 1, 2) as i:
                    chunk(i, 0)
                    chunk(i + 1, 1)
                last = NCH - 1
                nxt, st = f + 3 * NCH, 2 * l + 2
                split_his(nxt - 1)
                tanh(last, 0, 0)
                at_hi_evac(2 * last - 1, 1, 1 - last % 2, 1)
                split_his(nxt)
                at_hi_evac(2 * last, 0, last % 2, 0)
                split_his(nxt + 1)
                norm_squares(st, 0)
                split_his(nxt + 2)
                tanh(last, 1, 1)
                if l == 0:
                    norm_hi(st, 0, (0,))
                at_hi_evac(2 * last + 1, 1, last % 2, 1)
                if l == 0:
                    norm_hi(st, 0, (1,))
                split_his(nxt + 3)
                if l == 1:
                    last_scale(0)
                norm_squares(st, 1)
                if l == 1:
                    last_scale(1)

            act.dma_start(gain[0:1, :], norm_mix_g[0:1, :]).then_inc(gain_loaded, 16)
            norm_squares(0, 0)
            part_his(0)
            norm_hi(0, 0)
            split_his(0, 1, 2)
            norm_squares(0, 1)
            split_his(3)
            norm_hi(0, 1)
            mix0_act()
            ffn_act(0)
            mix1_act()
            ffn_act(1)

        @block.vector
        def _(dve):
            V = nc.vector
            chain = [0]

            def link(ins):
                chain[0] += 1
                ins.then_inc(dve_chain, 1)
                dve.wait_ge(dve_chain, chain[0])

            def split_lo(s, static=None):
                t = s if static is None else static
                parted = static is None and s < PARTED
                if parted and s:
                    part_los(s)
                dve.wait_ge(hi_ready, s + 1)
                c = slice(SLAB // 2 if parted else 0, SLAB)
                V.tensor_tensor(w_lo[:, t % SLOTS, c], raw[:, t % RAW_SLOTS, c],
                                w_hi[:, t % SLOTS, c].bitcast(F32), ALU.subtract).then_inc(lo_ready, 1)

            def part_los(s):
                dve.wait_ge(part_hi, s + 1)
                c = slice(0, SLAB // 2)
                V.tensor_tensor(w_lo[:, s, c], raw[:, s % RAW_SLOTS, c], w_hi[:, s, c].bitcast(F32), ALU.subtract)\
                    .then_inc(part_lo, 1)

            def split_los(*slabs):
                for s in slabs:
                    if s < SLABS:
                        split_lo(s)

            def norm_add(st, half):
                for b in range(2):
                    if half and b:
                        dve.wait_ge(slab_used, (ffn0[0], mix0[1], ffn0[1], SLABS)[st - 1])
                    else:
                        dve.wait_ge(acc_done, 3 * (st - 1) + 2 * half + b + 1)
                    hp = h[:, half, b * HALFD:(b + 1) * HALFD]
                    V.tensor_tensor(hp, bank[:, 2 * half + b, :], hp, ALU.add).then_inc(h_added, 1)
                    if st == 4:
                        dve.wait_ge(gain_loaded, 16 * (st + 1))
                        dve.wait_ge(h_added, 4 * (st - 1) + 2 * half + b + 1)
                        if half:
                            dve.wait_ge((normed, last_scaled)[b], (17, 1)[b])
                        V.tensor_tensor(gained[:, b, :], hp, gain[:, b * HALFD:(b + 1) * HALFD],
                                        ALU.mult).then_inc(gain_used, 1)

            def norm_scale(st, half):
                n = 4 * st + 2 * half
                dve.wait_ge(squared, n + 1)
                link(V.tensor_scalar(meansq[:, half:half + 1], sumsq[:, 2 * half:2 * half + 1],
                                     D * EPS, None, ALU.add))
                dve.wait_ge(squared, n + 2)
                V.tensor_scalar(meansq[:, half:half + 1], meansq[:, half:half + 1],
                                sumsq[:, 2 * half + 1:2 * half + 2], 1.0 / D, ALU.add, ALU.mult)\
                    .then_inc(pow_asked, 1)
                dve.wait_ge(pow_done, pow_no("norm", st, half))
                if st:
                    dve.wait_ge(gain_loaded, 16 * (st + 1))
                if st == 4:
                    V.tensor_scalar(h[:, half, 0:HALFD], gained[:, 0, :], rstd[:, half:half + 1], None,
                                    ALU.mult).then_inc(normed, 1)
                    return
                for b in range(2):
                    if st == 0:
                        dve.wait_ge(gain_spread, b + 1)
                    c = slice(b * HALFD, (b + 1) * HALFD)
                    g = gain[:, c] if st else bank[:, b, :]
                    V.scalar_tensor_tensor(xn[:, c], h[:, half, c], rstd[:, half:half + 1], g,
                                           ALU.mult, ALU.mult).then_inc(normed, 1)

            def norm_lo(st, half, blocks=(0, 1)):
                for b in blocks:
                    dve.wait_ge(xt_hi, 4 * st + 2 * half + b + 1)
                    hi = xT_hi[:, half, 4 * b:4 * b + 4, :].rearrange("p k t -> p (k t)")
                    lo = xT_lo[:, half, 4 * b:4 * b + 4, :].rearrange("p k t -> p (k t)")
                    V.tensor_tensor(lo, bank[:, 6 + b, :], hi.bitcast(F32), ALU.subtract).then_inc(xt_lo, 1)

            def k_evac(g):
                dve.wait_ge(slab_used, mix0[0] + NAT[0] + 2 * g + 2)
                for i in range(2):
                    r = slice(64 * i, 64 * i + 64)
                    last = V.tensor_copy(kT[r, i, :, :].rearrange("p s t -> p (s t)"), bank[r, 5, :])
                last.then_inc(k_copied, 1)

            def maxima(l, j):
                g, maps = 3 * l + j, 4 if l == 0 else 2
                scale = float(64 if l == 0 else 128) ** -0.5
                b0, *b1 = SCORE_BANKS[j]
                dve.wait_ge(scored, g + 1)
                link(V.reduce_max(rmax[:, 0:maps], bank[:, b0, 0:maps * P].rearrange("p (m k) -> p m k", m=maps),
                                  AX_X))
                V.tensor_scalar(nmax[:, 0:maps], rmax[:, 0:maps], -scale, None, ALU.mult).then_inc(nmax_ready, 1)
                for i in range(maps // 2):
                    last = V.reduce_max(rmax[:, 4 + 2 * i:6 + 2 * i],
                                        bank[:, b1[i], :].rearrange("p (m k) -> p m k", m=2), AX_X)
                link(last)
                V.tensor_scalar(nmax[:, 4:4 + maps], rmax[:, 4:4 + maps], -scale, None, ALU.mult)\
                    .then_inc(nmax_ready, 1)

            def combine(j):
                for q, pq in ((0, p0), (1, p1)):
                    dve.wait_ge(exp_done, 2 * j + q + 1)
                    c = slice(4 * q, 4 * q + 4)
                    link(V.reciprocal(rsum[:, c], sums[:, c]))
                    link(V.tensor_tensor(rsum[:, c], rsum[:, c], coef[:, c], ALU.mult))
                    for hd in range(2):
                        last = V.tensor_scalar(pq[:, 2 * hd, :], pq[:, 2 * hd, :],
                                               rsum[:, 4 * q + 2 * hd:4 * q + 2 * hd + 1], None, ALU.mult)
                    link(last)
                    for hd in range(2):
                        last = V.scalar_tensor_tensor(
                            pq[:, 2 * hd, :], pq[:, 2 * hd + 1, :],
                            rsum[:, 4 * q + 2 * hd + 1:4 * q + 2 * hd + 2], pq[:, 2 * hd, :], ALU.mult, ALU.add)
                last.then_inc(probs_ready, 1)

            def normalize(j):
                dve.wait_ge(exp_done, 2 * (3 + j) + 2)
                both = lambda t: t[:, :].rearrange("p (q m) -> p q m", q=2)[:, :, 0:2]
                link(V.reciprocal(both(rsum), both(sums)))
                for q, pq in ((0, p0), (1, p1)):
                    for hd in range(2):
                        last = V.tensor_scalar(pq[:, hd, :], pq[:, hd, :], rsum[:, 4 * q + hd:4 * q + hd + 1],
                                               None, ALU.mult)
                last.then_inc(probs_ready, 1)

            def probT_evac(j):
                dve.wait_ge(prob_t, 2 * j + 2)
                V.tensor_copy(probT[:, 1, :, :].rearrange("p b q -> p (b q)"),
                              bank[:, PROB_T_BANKS[j][1], 0:3 * P]).then_inc(probT_b, 1)

            def o_norm(j):
                dve.wait_ge(o_squared, j + 1)
                V.tensor_scalar(osq[:, :], osq[:, :], 1.0 / HD, EPS, ALU.mult, ALU.add).then_inc(pow_asked, 1)
                dve.wait_ge(pow_done, pow_no("head", j))
                for i in range(4):
                    last = V.scalar_tensor_tensor(o_sb[:, i // 2, i % 2, :], bank[:, OUT_BANK[j], i * P:(i + 1) * P],
                                                  osq[:, i:i + 1], subg[:, :], ALU.mult, ALU.mult)
                last.then_inc(o_ready, 1)

            def y_lo_evac(l, j):
                dve.wait_ge(y_hi, 3 * l + j + 1)
                V.tensor_tensor(yT_lo[:, :, 2 + 2 * j:4 + 2 * j, :],
                                bank[:, Y_BANK[l][j], :].rearrange("p (h k t) -> p h k t", h=2, k=2),
                                yT_hi[:, :, 2 + 2 * j:4 + 2 * j, :].bitcast(F32), ALU.subtract).then_inc(y_lo, 1)

            def prepare():
                dve.wait_ge(params_loaded, 64)
                prod = lam_in[:, :, :].rearrange("p (a b) n -> p a b n", b=2)
                link(V.tensor_tensor(prod[:, :, 0, :], prod[:, :, 0, :], prod[:, :, 1, :], ALU.mult))
                V.reduce_sum(lam_t[:, 0:2], prod[:, :, 0, :], AX_X).then_inc(lam_exp, 1)
                link(V.memset(coef[:, :], 1.0))
                V.memset(kT[64:P, 0, :, :], 0.0)
                link(V.memset(kT[0:64, 1, :, :], 0.0))
                link(V.tensor_scalar(subg[:, :], subg[:, :], 1.0 - LAM_INIT, None, ALU.mult))
                link(V.tensor_scalar(chan_half[:, :, :], chan[:, :, TAPS + 1:TAPS + 3], 0.5, None, ALU.mult))

            def lambda_coef():
                dve.wait_ge(lam_exp, 2)
                link(V.tensor_scalar(lam_t[:, 0:1], lam_t[:, 3:4], lam_t[:, 2:3], -LAM_INIT,
                                     ALU.subtract, ALU.add))
                odd = coef[:, :].rearrange("p (a b) -> p a b", b=2)[:, :, 1]
                link(V.tensor_scalar(odd, odd, lam_t[:, 0:1], None, ALU.mult))

            def mix0_dve():
                prepare()
                split_los(4, 5, 6, 7)
                lambda_coef()
                k_evac(0)
                split_los(8)
                maxima(0, 0)
                split_los(9)
                combine(0)
                split_los(10)
                probT_evac(0)
                k_evac(1)
                split_los(11)
                o_norm(0)
                maxima(0, 1)
                split_los(12)
                combine(1)
                split_los(13)
                k_evac(2)
                probT_evac(1)
                y_lo_evac(0, 0)
                dve.wait_ge(branch_act, 4)
                for c in range(2):
                    last = V.scalar_tensor_tensor(
                        yT_lo[:, :, c, :], bank[:, POOL_BANK, c * 256:(c + 1) * 256].rearrange("p (h t) -> p h t", h=2),
                        chan[:, c, TAPS + 3:TAPS + 4], yT_hi[:, :, c, :].bitcast(F32), ALU.mult, ALU.subtract)
                last.then_inc(branch_lo, 1)
                o_norm(1)
                maxima(0, 2)
                y_lo_evac(0, 1)
                combine(2)
                probT_evac(2)
                split_los(14)
                o_norm(2)
                y_lo_evac(0, 2)
                split_los(15)

            conv_n = [0]

            def conv(n):
                for _ in range(n):
                    k = conv_n[0]
                    if k >= 2 * TAPS:
                        return
                    tap, c = divmod(k, 2)
                    src = conv_in[:, c, tap:tap + SEQ]
                    w = chan[:, c, tap:tap + 1]
                    if tap == 0:
                        V.tensor_scalar(conv_acc[:, c, :], src, w, chan[:, c, TAPS:TAPS + 1], ALU.mult, ALU.add)\
                            .then_inc(conv_step, 1)
                    else:
                        dve.wait_ge(conv_step, k - 1)
                        V.scalar_tensor_tensor(conv_acc[:, c, :], src, w, conv_acc[:, c, :],
                                               ALU.mult, ALU.add).then_inc(conv_step, 1)
                    conv_n[0] += 1

            def mix1_dve():
                m, o, f = mix0[1], out0[1], ffn0[1]

                def gated_branch(half):
                    dve.wait_ge(branch_act, 4 + half + 1)
                    V.scalar_tensor_tensor(tmp_a[:, half, :], tmp_t[:, half, :], 1.0, bank[:, 4, 0:256],
                                           ALU.add, ALU.mult).then_inc(branch_dve, 1)

                V.memset(conv_in[:, :, 0:PAD], 0.0).then_inc(branch_dve, 1)
                gated_branch(0)
                split_los(m + 4)
                norm_lo(2, 1)
                split_los(m + 5, m + 6)
                gated_branch(1)
                split_los(m + 7, m + 8)
                dve.wait_ge(branch_act, 7)
                dve.wait_ge(branch_dve, 3)
                conv(6)
                split_los(m + 9)
                conv(8)
                split_los(m + 10)
                conv(12)
                maxima(1, 0)
                split_los(o)
                conv(10)
                normalize(0)
                split_los(o + 1)
                conv(12)
                y_lo_evac(1, 0)
                conv(4)
                maxima(1, 1)
                conv(4)
                normalize(1)
                conv(2 * TAPS)
                split_los(o + 2, o + 3)
                y_lo_evac(1, 1)
                maxima(1, 2)
                dve.wait_ge(branch_t, 5)
                for half in range(HALVES):
                    last = V.bn_stats(stats[:, half, :], bank[:, 5, half * 256:(half + 1) * 256])
                link(last)
                for half in range(HALVES):
                    last = V.bn_aggr(mv[:, half, :], stats[:, half, :])
                link(last)
                V.tensor_scalar(meansq[:, 2:4], mv[:, :, 1], EPS, None, ALU.add).then_inc(pow_asked, 1)
                normalize(2)
                dve.wait_ge(pow_done, pow_no("ln", 0))
                for half in range(HALVES):
                    last = V.tensor_scalar(ln[:, half, :], bank[:, 5, half * 256:(half + 1) * 256],
                                           mv[:, half, 0:1], rstd[:, 2 + half:3 + half], ALU.subtract, ALU.mult)
                last.then_inc(branch_dve, 1)
                split_los(f, f + 1)
                y_lo_evac(1, 2)
                dve.wait_ge(branch_act, 9)
                for c in range(2):
                    last = V.tensor_scalar(conv_acc[:, c, :], bank[:, 5, c * 256:(c + 1) * 256],
                                           chan[:, c, TAPS + 1:TAPS + 2], chan[:, c, TAPS + 2:TAPS + 3],
                                           ALU.mult, ALU.add)
                link(last)
                V.scalar_tensor_tensor(conv_acc[:, :, :], conv_in[:, :, 0:SEQ], 1.0, conv_acc[:, :, :],
                                       ALU.add, ALU.mult).then_inc(branch_dve, 1)
                dve.wait_ge(branch_act, 10)
                dve.wait_ge(branch_dve, CONV_SWISHED)
                for half in range(HALVES):
                    last = V.scalar_tensor_tensor(
                        yT_lo[:, half, 0:2, :], conv_acc[:, :, half * P:(half + 1) * P], 0.5,
                        yT_hi[:, half, 0:2, :].bitcast(F32), ALU.mult, ALU.subtract)
                last.then_inc(branch_lo, 1)

            def ffn_dve(l):
                U = 2 * NCH * l

                def activate(n, p):
                    dve.wait_ge(tanh_done, U + n + 1)
                    V.scalar_tensor_tensor(tmp_a[:, p, :], tmp_t[:, p, :], 1.0, bank[:, 4 + p, 0:256],
                                           ALU.add, ALU.mult).then_inc(gated, 1)
                    dve.wait_ge(gated, U + n + 1)
                    V.scalar_tensor_tensor(tmp_a[:, p, :], tmp_a[:, p, :], 0.5, bank[:, 4 + p, 256:512],
                                           ALU.mult, ALU.mult).then_inc(act_ready, 1)

                def at_lo_evac(n, np_, ip, half):
                    dve.wait_ge(at_hi, U + n + 1)
                    hi = actT_hi[:, half, 2 * ip:2 * ip + 2, :].rearrange("p k t -> p (k t)")
                    lo = actT_lo[:, half, 2 * ip:2 * ip + 2, :].rearrange("p k t -> p (k t)")
                    V.tensor_tensor(lo, bank[:, 6 + np_, 0:256], hi.bitcast(F32), ALU.subtract).then_inc(at_lo, 1)

                f = ffn0[l]
                if l == 1:
                    split_los(f + 2)
                norm_add(2 * l + 1, 0)
                norm_scale(2 * l + 1, 0)
                if l == 0:
                    split_los(f + 2)
                norm_lo(2 * l + 1, 0)
                norm_add(2 * l + 1, 1)
                norm_scale(2 * l + 1, 1)
                split_los(f + 3)
                activate(0, 0)
                norm_lo(2 * l + 1, 1)
                split_los(f + 4)
                activate(1, 1)
                at_lo_evac(0, 0, 0, 0)
                split_los(f + 5)
                activate(2, 0)
                split_los(f + 6, f + 7)
                at_lo_evac(1, 1, 1, 0)
                activate(3, 1)
                at_lo_evac(2, 0, 0, 1)

                def chunk(i, p):
                    s = up_slab(l, i) + 3
                    static = up_slab(l, 2 + p) + 3
                    split_lo(s, static)
                    activate(2 * i, 0)
                    at_lo_evac(2 * i - 1, 1, 1 - p, 1)
                    split_lo(s + 1, static + 1)
                    activate(2 * i + 1, 1)
                    at_lo_evac(2 * i, 0, p, 0)
                    split_lo(s + 2, static + 2)

                with dve.Fori(2, NCH - 1, 2) as i:
                    chunk(i, 0)
                    chunk(i + 1, 1)
                last = NCH - 1
                nxt, st = f + 3 * NCH, 2 * l + 2
                split_los(nxt - 1)
                activate(2 * last, 0)
                at_lo_evac(2 * last - 1, 1, 1 - last % 2, 1)
                at_lo_evac(2 * last, 0, last % 2, 0)
                split_los(nxt)
                norm_add(st, 0)
                norm_scale(st, 0)
                split_los(nxt + 1)
                activate(2 * last + 1, 1)
                if l == 0:
                    norm_lo(st, 0, (0,))
                at_lo_evac(2 * last + 1, 1, last % 2, 1)
                if l == 0:
                    norm_lo(st, 0, (1,))
                split_los(nxt + 2)
                norm_add(st, 1)
                norm_scale(st, 1)
                split_los(nxt + 3)

            norm_scale(0, 0)
            part_los(0)
            norm_lo(0, 0)
            split_los(0, 1, 2)
            norm_scale(0, 1)
            split_los(3)
            norm_lo(0, 1)
            mix0_dve()
            ffn_dve(0)
            mix1_dve()
            ffn_dve(1)

        @block.tensor
        def _(pe):
            T = nc.tensor

            def keep_warm(n):
                for _ in range(n):
                    T.transpose(bank[:, 5, 0:P], ident[:, :], ident[:, :])

            def split_product(o, st_hi, st_lo, mv_hi, mv_lo, first, last):
                T.matmul(o, st_hi, mv_lo, start=first, stop=False)
                T.matmul(o, st_hi, mv_hi, start=False, stop=False)
                return T.matmul(o, st_lo, mv_hi, start=False, stop=last)

            def w_part(s, c0, n):
                return w_hi[:, slot(s), c0:c0 + n], w_lo[:, slot(s), c0:c0 + n]

            def unit(s, static, half, b, width=512, slabs=2, release=False, done=None, st=None,
                     midway=None):
                per = KC // slabs
                for k in range(KC):
                    if k == KC // 2 and midway:
                        midway()
                    if st is not None and k % 4 == 0:
                        pe.wait_ge(xt_lo, 4 * st + 2 * half + k // 4 + 1)
                    if not in_register(s) and s < PARTED and half == 0:
                        if k % 4 == 0:
                            pe.wait_ge(part_lo, s + k // 4 + 1)
                        elif k % 4 == 2:
                            pe.wait_ge(lo_ready, s + k // 4 + 1)
                    elif k % per == 0:
                        pe.wait_ge(lo_ready, s + k // per + 1)
                    hi, lo = w_part(static + k // per, (k % per) * width, width)
                    last = split_product(bank[:, b, 0:width], xT_hi[:, half, k, :], xT_lo[:, half, k, :],
                                         hi, lo, k == 0, k == KC - 1)
                    if release and k % per == per - 1:
                        last.then_inc(slab_used, 1)
                if not release:
                    last.then_inc(done, 1)

            def norm_transposes(st, half, blocks=(0, 1)):
                for b in blocks:
                    pe.wait_ge(normed, 4 * st + 2 * half + b + 1)
                    if half:
                        pe.wait_ge(xt_lo, 4 * st + b + 1)
                    for k in range(4):
                        last = T.transpose(bank[:, 6 + b, k * P:(k + 1) * P], xn[:, (4 * b + k) * P:(4 * b + k + 1) * P],
                                           ident[:, :])
                    last.then_inc(normed_t, 1)

            def qk_chunk(l, j):
                s = mix0[l] + NAT[l] + 2 * j
                pe.wait_ge(lo_ready, s + 2)
                for sub in range(4):
                    if j == 0 and sub % 2 == 0:
                        pe.wait_ge(nat_copied, (3, 7)[l] + sub // 2)
                    for k in range(KC):
                        hi, lo = w_part(s + k // 4, (k % 4) * 512 + sub * P, P)
                        last = split_product(bank[:, 4 + sub // 2, (sub % 2) * 256:(sub % 2) * 256 + 256],
                                             hi, lo, xT_hi[:, :, k, :], xT_lo[:, :, k, :], k == 0, k == KC - 1)
                        if sub == 3 and k % 4 == 3:
                            last.then_inc(slab_used, 1)
                    if sub == 1:
                        last.then_inc(q_done, 1)

            def scores(l, j):
                g, maps = 3 * l + j, 4 if l == 0 else 2
                b0, *b1 = SCORE_BANKS[j]
                pe.wait_ge(q_copied, g + 1)
                if l == 0:
                    pe.wait_ge(k_copied, j + 1)
                if g == 0:
                    pe.wait_ge(consts, MASK_MADE)
                at = maps // 2
                keys = [kT[:, 0:at, sub, :] for sub in range(2)]
                by_map = lambda b, n: bank[:, b, 0:maps * n].rearrange("p (m k) -> p m k", m=maps)
                T.matmul(by_map(b0, P), ident_b[:, :], mask_b[:, 0:maps, :], start=True, stop=False)
                for sub in range(2):
                    T.matmul(by_map(b0, P)[:, at * sub:at * sub + at, :], qT[:, sub, 0:P], keys[sub][:, :, 0:P],
                             start=False, stop=sub == 1)
                for sub in range(2):
                    b, c = (b1[sub], 0) if l == 0 else (b1[0], 256 * sub)
                    T.matmul(bank[:, b, c:c + 256 * at], qT[:, sub, P:2 * P], keys[sub],
                             start=l == 0 or sub == 0, stop=False)
                for b in b1[0:at]:
                    last = T.matmul(bank[:, b, :].rearrange("p (m k) -> p m k", m=2)[:, :, P:2 * P],
                                    ident_b[:, :], mask_b[:, 0:2, :], start=False, stop=True)
                last.then_inc(scored, 1)

            def attend(l, j, between=None):
                g = 3 * l + j
                step = 2 if l == 0 else 1
                pe.wait_ge(probs_ready, g + 1)
                if j == 2:
                    pe.wait_ge(y_lo, g)
                for hd in range(2):
                    b = PROB_T_BANKS[j][hd]
                    m = step * hd
                    for i, src in enumerate((p0[:, m, :], p1[:, m, 0:P], p1[:, m, P:2 * P])):
                        last = T.transpose(bank[:, b, i * P:(i + 1) * P], src, ident[:, :])
                    last.then_inc(prob_t, 1)
                if between:
                    between()
                for hd in range(2):
                    if l == 0:
                        pe.wait_ge((probT_a, probT_b)[hd], j + 1)
                    else:
                        pe.wait_ge(probT_a, 3 + 2 * j + hd + 1)
                    head = slice((2 * j + hd) * P, (2 * j + hd + 1) * P)
                    if l == 0:
                        o = bank[:, OUT_BANK[j], hd * P:(hd + 1) * P]
                        T.matmul(o, probT[:, hd, 0, :], v[:, 0, head], start=True, stop=True)
                        o = bank[:, OUT_BANK[j], (2 + hd) * P:(3 + hd) * P]
                        T.matmul(o, probT[:, hd, 1, :], v[:, 0, head], start=True, stop=False)
                        last = T.matmul(o, probT[:, hd, 2, :], v[:, 1, head], start=False, stop=True)
                    else:
                        o = bank[:, Y_BANK[1][j], :].rearrange("p (h k t) -> p h k t", h=2, k=2)[:, :, hd, :]
                        T.matmul(o, v[:, 0, head], probT[:, hd, 0:2, :], start=True, stop=False)
                        last = T.matmul(o[:, 1, :], v[:, 1, head], probT[:, hd, 2, :], start=False, stop=True)
                last.then_inc(o_done if l == 0 else y_t, 1)

            def y_transposes(j):
                pe.wait_ge(o_ready, j + 1)
                for i in range(4):
                    last = T.transpose(bank[:, Y_BANK[0][j], i * P:(i + 1) * P], o_sb[:, i // 2, i % 2, :], ident[:, :])
                last.then_inc(y_t, 1)

            def rows_product(s, static, half, b, act_hi, act_lo, first, last_slab):
                pe.wait_ge(lo_ready, s + 1)
                for k in range(2):
                    hi, lo = w_part(static, k * D + b * HALFD, HALFD)
                    last = split_product(bank[:, 2 * half + b, :], act_hi[:, k, :], act_lo[:, k, :],
                                         hi, lo, first and k == 0, last_slab and k == 1)
                if half and b:
                    last.then_inc(slab_used, 1)
                elif last_slab:
                    last.then_inc(acc_done, 1)

            def out_slab(l, o, half, blocks=(0, 1)):
                k0 = OUT_ROWS[l][o]
                for b in blocks:
                    if k0:
                        pe.wait_ge(y_lo, 3 * l + k0 // 2)
                    else:
                        pe.wait_ge(branch_lo, l + 1)
                    if l == 0 and o == 0 and half == 0 and b:
                        pe.wait_ge(branch_lo, 1)
                    rows_product(out0[l] + o, out0[l] + o, half, b, yT_hi[:, half, k0:k0 + 2, :],
                                 yT_lo[:, half, k0:k0 + 2, :], o == 0, o == 3)

            def pool_differences():
                pe.wait_ge(consts, CONSTS_MADE)
                for g in range(4):
                    b, c = 6 + g // 2, 256 * (g % 2)
                    ch = slice(g * 64, (g + 1) * 64)
                    T.matmul(bank[0:64, b, c:c + 256], u_sb[:, 0, ch], branch[:, g, 0:256], start=True, stop=False)
                    last = T.matmul(bank[0:64, b, c + P:c + 2 * P], u_sb[:, 1, ch], branch[:, g, 256:384],
                                    start=False, stop=True)
                    if g % 2:
                        last.then_inc(branch_t, 1)

            def pool_map():
                pe.wait_ge(branch_act, 2)
                for g in range(4):
                    r = slice(64 * (g % 2), 64 * (g % 2) + 64)
                    c = 256 * (g // 2)
                    last = T.matmul(bank[r, POOL_BANK, c:c + 256], pw_sb[:, g, :], dT[:, g, :], start=True, stop=True)
                last.then_inc(branch_t, 1)

            def gated_transposes():
                pe.wait_ge(branch_dve, 3)
                for c in range(2):
                    for half in range(HALVES):
                        last = T.transpose(bank[:, 6, c * 256 + half * P:c * 256 + (half + 1) * P],
                                           tmp_a[:, half, c * P:(c + 1) * P], ident[:, :])
                last.then_inc(branch_t, 1)

            def conv_transposes():
                pe.wait_ge(conv_step, 2 * TAPS)
                pe.wait_ge(q_copied, 6)
                for half in range(HALVES):
                    for c in range(2):
                        last = T.transpose(bank[:, 5, half * 256 + c * P:half * 256 + (c + 1) * P],
                                           conv_acc[:, c, half * P:(half + 1) * P], ident[:, :])
                last.then_inc(branch_t, 1)

            def layer_norm_transposes():
                pe.wait_ge(branch_dve, 4)
                for c in range(2):
                    for half in range(HALVES):
                        last = T.transpose(bank[:, 5, c * 256 + half * P:c * 256 + (half + 1) * P],
                                           ln[:, half, c * P:(c + 1) * P], ident[:, :])
                last.then_inc(branch_t, 1)

            def mix(l):
                st, m = 2 * l, mix0[l]
                unit(m, m, 0, 4, done=nat_done, st=st)
                unit(m + 2, m + 2, 0, 5, done=nat_done, midway=lambda: norm_transposes(st, 1))
                if l == 0:
                    pe.wait_ge(nat_copied, 1)
                else:
                    pe.wait_ge(branch_dve, 2)
                unit(m, m, 1, 4, release=True, st=st)
                pe.wait_ge(nat_copied, 2 if l == 0 else 5)
                unit(m + 2, m + 2, 1, 5, release=True)
                if l == 1:
                    gated_transposes()
                    unit(m + 4, m + 4, 0, 4, 256, 1, done=nat_done)
                    pe.wait_ge(nat_copied, 6)
                    unit(m + 4, m + 4, 1, 5, 256, 1, release=True)
                qk_chunk(l, 0)
                if l == 0:
                    pool_differences()
                scores(l, 0)
                qk_chunk(l, 1)
                if l == 0:
                    attend(l, 0)
                    scores(l, 1)
                else:
                    attend(l, 0, lambda: scores(l, 1))
                qk_chunk(l, 2)
                if l == 0:
                    y_transposes(0)
                    attend(l, 1, pool_map)
                    scores(l, 2)
                    out_slab(l, 0, 0, (0,))
                    y_transposes(1)
                    out_slab(l, 0, 0, (1,))
                    out_slab(l, 0, 1)
                    out_slab(l, 1, 0, (0,))
                    attend(l, 2, lambda: out_slab(l, 1, 0, (1,)))
                    out_slab(l, 2, 0)
                    out_slab(l, 1, 1, (0,))
                    y_transposes(2)
                    out_slab(l, 1, 1, (1,))
                    out_slab(l, 3, 0)
                    out_slab(l, 2, 1)
                    out_slab(l, 3, 1, (0,))
                    norm_transposes(st + 1, 0, (0,))
                    out_slab(l, 3, 1, (1,))
                    norm_transposes(st + 1, 0, (1,))
                else:
                    attend(l, 1, conv_transposes)
                    scores(l, 2)
                    out_slab(l, 0, 0)
                    out_slab(l, 0, 1)
                    attend(l, 2, lambda: out_slab(l, 1, 0, (0,)))
                    out_slab(l, 1, 0, (1,))
                    layer_norm_transposes()
                    out_slab(l, 1, 1, (0,))
                    out_slab(l, 1, 1, (1,))
                    out_slab(l, 2, 0)
                    out_slab(l, 3, 0)
                    out_slab(l, 2, 1)
                    out_slab(l, 3, 1, (0,))
                    norm_transposes(st + 1, 0, (0,))
                    out_slab(l, 3, 1, (1,))
                    norm_transposes(st + 1, 0, (1,))

            def ffn(l):
                U, f = 2 * NCH * l, ffn0[l]

                def up(i, half, n, static, st=None, midway=None):
                    if in_register(n) or n >= 2:
                        pe.wait_ge(act_ready, U + n - 1)
                    unit(up_slab(l, i), static, half, 4 + (half if in_register(i) or i >= 2 else i),
                         release=half == 1, done=up_done, st=st, midway=midway)

                def transposes(n, p):
                    pe.wait_ge(act_ready, U + n + 1)
                    if in_register(n) or n >= 2:
                        pe.wait_ge(at_lo, U + n - 1)
                    for k in range(2):
                        last = T.transpose(bank[:, 6 + p, k * P:(k + 1) * P], tmp_a[:, p, k * P:(k + 1) * P],
                                           ident[:, :])
                    last.then_inc(act_t, 1)

                def down(i, n, static, half, ip, first=False, final=False, between=None):
                    pe.wait_ge(at_lo, U + n + 1)
                    for b in range(2):
                        rows_product(down_slab(l, i), static, half, b, actT_hi[:, half, 2 * ip:2 * ip + 2, :],
                                     actT_lo[:, half, 2 * ip:2 * ip + 2, :], first, final)
                        if b == 0 and between:
                            between()

                st = 2 * l + 1
                up(0, 0, 0, f, st=st)
                up(1, 0, 1, f + 2, midway=lambda: norm_transposes(st, 1))
                pe.wait_ge(xt_lo, 4 * st + 3)
                transposes(0, 0)
                up(0, 1, 2, f, st=st)
                transposes(1, 1)
                up(1, 1, 3, f + 2)
                transposes(2, 0)
                down(0, 0, f + 4, 0, 0, first=True)
                down(0, 2, f + 4, 1, 0, first=True)

                def chunk(i, p):
                    su, sd = up_slab(l, 2 + p), down_slab(l, 1 + p)
                    up(i, 0, 2 * i, su)
                    transposes(2 * i - 1, 1)
                    down(i - 1, 2 * i - 2 if in_register(i) else unit_no(i - 1, 0), sd, 0, 1 - p)
                    up(i, 1, 2 * i + 1, su)
                    transposes(2 * i, 0)
                    down(i - 1, 2 * i - 1, sd, 1, 1 - p)

                with pe.Fori(2, NCH - 1, 2) as i:
                    chunk(i, 0)
                    chunk(i + 1, 1)
                e = NCH - 1
                up(e, 0, 2 * e, up_slab(l, e))
                transposes(2 * e - 1, 1)
                down(e - 1, 2 * e - 2, down_slab(l, e - 1), 0, (e - 1) % 2, between=lambda: transposes(2 * e, 0))
                down(e, 2 * e, down_slab(l, e), 0, e % 2, final=True)
                up(e, 1, 2 * e + 1, up_slab(l, e))
                if l == 0:
                    norm_transposes(st + 1, 0, (0,))
                down(e - 1, 2 * e - 1, down_slab(l, e - 1), 1, (e - 1) % 2, between=lambda: transposes(2 * e + 1, 1))
                pe.wait_ge(at_lo, U + 2 * e + 2)
                if l == 0:
                    norm_transposes(st + 1, 0, (1,))
                down(e, 2 * e + 1, down_slab(l, e), 1, e % 2, final=True)

            pe.wait_ge(consts, IDENT_MADE)
            keep_warm(8)
            pe.wait_ge(gain_loaded, 16)
            for b in range(2):
                T.matmul(bank[:, b, :], ones[:, :], gain[0:1, b * HALFD:(b + 1) * HALFD], start=True, stop=True)\
                    .then_inc(gain_spread, 1)
            norm_transposes(0, 0)
            keep_warm(5)
            for l in range(2):
                mix(l)
                ffn(l)


_INS = ["x", "norm_mix_g", "norm_ffn_g", "norm_final_g", "ab_w_in", "ab_w_out", "pool_w", "diff_lambda",
        "diff_subln_g", "cd_w_in", "cd_w_out", "channel_params", "ffn_w_gate", "ffn_w_up", "ffn_w_down"]


def kernel(**inputs):
    import numpy as _np
    import concourse.bacc as _bacc
    from concourse import mybir as _mybir
    from concourse.bass_utils import run_bass_kernel_spmd as _run

    a = {k: _np.ascontiguousarray(t) for k, t in inputs.items()}
    a["x"] = a["x"][0]
    a["norm_final_g"] = a["norm_final_g"].reshape(1, -1)
    for k in ("ab_w_in", "ab_w_out", "pool_w", "diff_lambda", "cd_w_in", "cd_w_out"):
        a[k] = a[k][0]
    a["channel_params"] = _np.concatenate(
        [a["conv_w"][0].T] + [a[k][0][:, None] for k in ("conv_b", "conv_ln_g", "conv_ln_b", "pool_scale")], axis=1)
    nc = _bacc.Bacc("TRN2", target_bir_lowering=False, num_devices=1)
    arrays, args = {}, []
    for name in _INS:
        t = _np.ascontiguousarray(a[name])
        arrays[f"in_{name}"] = t
        args.append(nc.dram_tensor(f"in_{name}", t.shape, _mybir.dt.from_np(t.dtype), kind="ExternalInput").ap())
    args.append(nc.dram_tensor("out", a["x"].shape, _mybir.dt.float32, kind="ExternalOutput").ap())
    trunk(nc, *args)
    r = _run(nc, [arrays], core_ids=[0])
    return r.results[0]["out"].reshape(inputs["x"].shape)
```
